# Optimizing a Trainium2 kernel written in Bass

```python
import jax, jax.numpy as jnp
from jax import lax
import numpy as np

D_MODEL = 2048
BATCH = 1
SEQ = 256
DEPTH = 2

N_MEM = 256
EPS = 1e-6
N_EVEN = (DEPTH + 1) // 2
N_ODD = DEPTH // 2

SB_HEADS = 4
SB_HEAD_DIM = 256
SB_WIDTH = SB_HEADS * SB_HEAD_DIM
SB_BLOCK = 128
SB_MASK_VALUE = -1e4
POOL_WINDOWS = (2, 4, 8, 16)
POOL_GROUPS = len(POOL_WINDOWS)
POOL_WIDTH = D_MODEL - SB_WIDTH
POOL_GROUP_DIM = POOL_WIDTH // POOL_GROUPS
EVEN_IN = 3 * SB_WIDTH + POOL_WIDTH

GLA_HEADS = 4
GLA_KEY_DIM = D_MODEL // 2
GLA_VAL_DIM = D_MODEL
GLA_HK = GLA_KEY_DIM // GLA_HEADS
GLA_HV = GLA_VAL_DIM // GLA_HEADS
GLA_GATE_RANK = 16
GLA_GATE_NORMALIZER = 16.0
GLA_CHUNK = 64
ODD_IN = 2 * GLA_KEY_DIM + 2 * GLA_VAL_DIM + GLA_GATE_RANK

X_HEADS = 4
X_HEAD_DIM = D_MODEL // X_HEADS

D_FF = -(-8 * D_MODEL // (3 * 256)) * 256

kernel_name = "stickbreak_pool_gla_hybrid_trunk"

F32 = jnp.float32

def rmsnorm(x, g):
    xf = x.astype(F32)
    y = xf * lax.rsqrt(jnp.mean(xf * xf, axis=-1, keepdims=True) + EPS)
    return (y * g.astype(F32)).astype(x.dtype)

def stick_breaking_attention(q, k, v):
    B, S, H, dh = q.shape
    C = SB_BLOCK
    nblk = S // C
    qh = q.transpose(0, 2, 1, 3).astype(F32) * (dh ** -0.5)
    kh = k.transpose(0, 2, 1, 3).astype(F32)
    vh = v.transpose(0, 2, 1, 3).astype(F32)
    ar = jnp.arange(C)
    later_in_block = (ar[:, None] > ar[None, :]).astype(F32)
    outs = []
    for i in range(nblk):
        nk = i + 1
        Lk = nk * C
        qb = qh[:, :, i * C:(i + 1) * C]
        kb = kh[:, :, :Lk]
        vb = vh[:, :, :Lk]
        z = jnp.einsum('bhqd,bhkd->bhqk', qb, kb)
        q_pos = i * C + ar
        mask = jnp.arange(Lk)[None, :] < q_pos[:, None]
        z = jnp.where(mask, z, SB_MASK_VALUE).reshape(B, H, C, nk, C)
        log_stay = jax.nn.log_sigmoid(-z)
        within = jnp.einsum('bhqcj,js->bhqcs', log_stay, later_in_block)
        blk_tot = jnp.sum(log_stay, axis=-1)
        bi = jnp.arange(nk)
        later_blocks = (bi[:, None] > bi[None, :]).astype(F32)
        after = jnp.einsum('bhqc,cd->bhqd', blk_tot, later_blocks)
        w = jnp.exp(z + log_stay + within + after[..., None]).reshape(B, H, C, Lk)
        outs.append(jnp.einsum('bhqk,bhkd->bhqd', w, vb))
    out = jnp.concatenate(outs, axis=2)
    return out.transpose(0, 2, 1, 3).astype(q.dtype)

def multiscale_pool(u, pool_w, pool_scale):
    B, S, C = u.shape
    groups = u.astype(F32).reshape(B, S, POOL_GROUPS, POOL_GROUP_DIM)
    cs = lax.associative_scan(jnp.add, groups, axis=1)
    pos = jnp.arange(S)
    pooled = []
    for gi, w in enumerate(POOL_WINDOWS):
        cg = cs[:, :, gi]
        shifted = jnp.pad(cg[:, :S - w], ((0, 0), (w, 0), (0, 0)))
        count = jnp.minimum(pos + 1, w).astype(F32)
        mean = (cg - shifted) / count[None, :, None]
        pooled.append(mean - groups[:, :, gi])
    p = jnp.stack(pooled, axis=2)
    y = jnp.einsum('bsgc,gcd->bsgd', p, pool_w.astype(F32)).reshape(B, S, C)
    return (y * pool_scale.astype(F32)).astype(u.dtype)

def gla_chunked(q, k, v, g):
    B, S, H, dk = q.shape
    dv = v.shape[-1]
    L = GLA_CHUNK
    n = S // L

    def chunks(t):
        return t.astype(F32).reshape(B, n, L, H, t.shape[-1]).transpose(0, 3, 1, 2, 4)

    q = chunks(q) * (dk ** -0.5)
    k = chunks(k)
    v = chunks(v)
    b = jnp.cumsum(chunks(g), axis=3)
    b_ref = b[:, :, :, L // 2:L // 2 + 1]
    b_last = b[:, :, :, L - 1:]

    qi = q * jnp.exp(b - b_ref)
    ki = k * jnp.exp(b_ref - b)
    scores = jnp.einsum('bhnld,bhnmd->bhnlm', qi, ki)
    causal = jnp.tril(jnp.ones((L, L), dtype=bool))
    scores = jnp.where(causal, scores, 0.0)
    o_intra = jnp.einsum('bhnlm,bhnme->bhnle', scores, v)

    q_inter = q * jnp.exp(b)
    k_state = k * jnp.exp(b_last - b)
    decay = jnp.exp(b_last[..., 0, :])

    def step(state, xs):
        qc, kc, vc, dc = xs
        o = jnp.einsum('bhld,bhde->bhle', qc, state)
        state = dc[..., None] * state + jnp.einsum('bhld,bhle->bhde', kc, vc)
        return state, o

    xs = (jnp.moveaxis(q_inter, 2, 0), jnp.moveaxis(k_state, 2, 0),
          jnp.moveaxis(v, 2, 0), jnp.moveaxis(decay, 2, 0))
    state0 = jnp.zeros((B, H, dk, dv), F32)
    _, o_inter = lax.scan(step, state0, xs)
    o = o_intra + jnp.moveaxis(o_inter, 0, 2)
    return o.transpose(0, 2, 3, 1, 4).reshape(B, S, H, dv)

def even_mixer(h, w_in, pool_w, pool_scale, w_out):
    B, S, _ = h.shape
    proj = h @ w_in
    q, k, v, u = jnp.split(proj, [SB_WIDTH, 2 * SB_WIDTH, 3 * SB_WIDTH], axis=-1)
    shp = (B, S, SB_HEADS, SB_HEAD_DIM)
    o_sb = stick_breaking_attention(q.reshape(shp), k.reshape(shp), v.reshape(shp))
    o_pool = multiscale_pool(u, pool_w, pool_scale)
    return jnp.concatenate([o_sb.reshape(B, S, SB_WIDTH), o_pool], axis=-1) @ w_out

def odd_mixer(h, w_in, gate_w, gate_b, gnorm, w_out):
    B, S, _ = h.shape
    proj = h @ w_in
    K, V = GLA_KEY_DIM, GLA_VAL_DIM
    q, k, v, r, a = jnp.split(proj, [K, 2 * K, 2 * K + V, 2 * K + 2 * V], axis=-1)
    g = jax.nn.log_sigmoid((a @ gate_w + gate_b).astype(F32)) / GLA_GATE_NORMALIZER
    o = gla_chunked(q.reshape(B, S, GLA_HEADS, GLA_HK), k.reshape(B, S, GLA_HEADS, GLA_HK),
                    v.reshape(B, S, GLA_HEADS, GLA_HV), g.reshape(B, S, GLA_HEADS, GLA_HK))
    o = rmsnorm(o, gnorm) * jax.nn.silu(r.reshape(B, S, GLA_HEADS, GLA_HV).astype(F32))
    return o.reshape(B, S, V).astype(h.dtype) @ w_out

def memory_cross_attention(h, mem_n, wq, wk, wv, wo):
    B, S, _ = h.shape
    M = mem_n.shape[1]
    q = (h @ wq).reshape(B, S, X_HEADS, X_HEAD_DIM)
    k = (mem_n @ wk).reshape(B, M, X_HEADS, X_HEAD_DIM)
    v = (mem_n @ wv).reshape(B, M, X_HEADS, X_HEAD_DIM)
    s = jnp.einsum('bshd,bmhd->bhsm', q, k).astype(F32) * (X_HEAD_DIM ** -0.5)
    p = jax.nn.softmax(s, axis=-1).astype(v.dtype)
    o = jnp.einsum('bhsm,bmhd->bshd', p, v).reshape(B, S, X_HEADS * X_HEAD_DIM)
    return o @ wo

def swiglu(h, w_gate, w_up, w_down):
    return (jax.nn.silu(h @ w_gate) * (h @ w_up)) @ w_down

def setup_inputs(seed: int = 0) -> dict:
    key = jax.random.key(seed)
    ks = jax.random.split(key, 20)

    def nrm(k, shape, fan_in):
        return jax.random.normal(k, shape, F32) * (fan_in ** -0.5)

    D = D_MODEL
    return {
        "x": jax.random.normal(ks[0], (BATCH, SEQ, D), F32),
        "mem": jax.random.normal(ks[1], (BATCH, N_MEM, D), F32),
        "norms": 1.0 + 0.1 * jax.random.normal(ks[2], (DEPTH, 6, D), F32),
        "mem_norm": 1.0 + 0.1 * jax.random.normal(ks[3], (D,), F32),
        "even_w_in": nrm(ks[4], (N_EVEN, D, EVEN_IN), D),
        "pool_w": nrm(ks[5], (N_EVEN, POOL_GROUPS, POOL_GROUP_DIM, POOL_GROUP_DIM), POOL_GROUP_DIM),
        "pool_scale": 1.0 + 0.1 * jax.random.normal(ks[6], (N_EVEN, POOL_WIDTH), F32),
        "even_w_out": nrm(ks[7], (N_EVEN, D, D), D),
        "odd_w_in": nrm(ks[8], (N_ODD, D, ODD_IN), D),
        "gla_gate_w": nrm(ks[9], (N_ODD, GLA_GATE_RANK, GLA_KEY_DIM), GLA_GATE_RANK),
        "gla_gate_b": 0.1 * jax.random.normal(ks[10], (N_ODD, GLA_KEY_DIM), F32),
        "gla_gnorm": 1.0 + 0.1 * jax.random.normal(ks[11], (N_ODD, GLA_HV), F32),
        "odd_w_out": nrm(ks[12], (N_ODD, GLA_VAL_DIM, D), GLA_VAL_DIM),
        "xattn_wq": nrm(ks[13], (DEPTH, D, D), D),
        "xattn_wk": nrm(ks[14], (DEPTH, D, D), D),
        "xattn_wv": nrm(ks[15], (DEPTH, D, D), D),
        "xattn_wo": nrm(ks[16], (DEPTH, D, D), D),
        "ffn_w_gate": nrm(ks[17], (DEPTH, D, D_FF), D),
        "ffn_w_up": nrm(ks[18], (DEPTH, D, D_FF), D),
        "ffn_w_down": nrm(ks[19], (DEPTH, D_FF, D), D_FF),
    }

def reference(x, mem, norms, mem_norm, even_w_in, pool_w, pool_scale, even_w_out,
              odd_w_in, gla_gate_w, gla_gate_b, gla_gnorm, odd_w_out,
              xattn_wq, xattn_wk, xattn_wv, xattn_wo,
              ffn_w_gate, ffn_w_up, ffn_w_down):
    mem_n = rmsnorm(mem, mem_norm)
    for layer in range(DEPTH):
        g = norms[layer]
        i = layer // 2
        h = rmsnorm(x, g[0])
        if layer % 2 == 0:
            mix = even_mixer(h, even_w_in[i], pool_w[i], pool_scale[i], even_w_out[i])
        else:
            mix = odd_mixer(h, odd_w_in[i], gla_gate_w[i], gla_gate_b[i], gla_gnorm[i], odd_w_out[i])
        x = x + rmsnorm(mix, g[1])
        h = rmsnorm(x, g[2])
        x = x + rmsnorm(memory_cross_attention(h, mem_n, xattn_wq[layer], xattn_wk[layer],
                                               xattn_wv[layer], xattn_wo[layer]), g[3])
        h = rmsnorm(x, g[4])
        x = x + rmsnorm(swiglu(h, ffn_w_gate[layer], ffn_w_up[layer], ffn_w_down[layer]), g[5])
    return x


_drawn_inputs = setup_inputs


def setup_inputs(seed=0):
    import zlib

    import numpy as np

    out = dict(_drawn_inputs(seed))
    spreads = {}
    factors = {}
    for name, (base, spread) in spreads.items():
        noise = np.random.default_rng([zlib.crc32(name.encode()), seed]).standard_normal(out[name].shape)
        drawn = base * np.exp(spread * noise) if base else spread * noise
        out[name] = __import__('jax').numpy.asarray(drawn.astype(out[name].dtype))
    for name, factor in factors.items():
        out[name] = (out[name] * factor).astype(out[name].dtype)
    return out
```

```python
from contextlib import ExitStack

import concourse.bass as bass
from concourse import mybir

F32 = mybir.dt.float32
F32R = mybir.dt.float32r
ALU = mybir.AluOpType
ACT = mybir.ActivationFunctionType
AX_X = mybir.AxisListType.X

P = 128
NB = 512
EPS = 1e-6
MASKED = -1e4
CHUNK = 2048
W_SLOTS = 4
RAW_SLOTS = 2
WORK = 4


def build(nc, x, mem, norms, mem_norm, even_w_in, pool_w, pool_scale, even_w_out, odd_w_in, gate_w,
          gate_b, gnorm, odd_w_out, wq, wk, wv, wo, w_gate, w_up, w_down, out):
    T, D = x.shape
    MT = T // P
    KT = D // P
    FF = w_gate.shape[2]
    FT = FF // P
    LAYERS = norms.shape[0]
    SBH, SBD = 4, 256
    SBW = SBH * SBD
    GH, GK, GV, CH = 4, 256, 512, 64
    NCH = T // CH
    RANK = gate_w.shape[0]
    XH, XD = 4, D // 4
    assert (T, D, MT, KT, LAYERS) == (256, 2048, 2, 16, 2) and FF % NB == 0

    plan = {}
    at = {"a": 0, "c": 0, "u": 0, "r": 0, "rf": 0}

    def stage(name, quads=0, rounds=0, down=False):
        plan[name] = dict(at)
        at["a"] += quads
        at["c"] += 4 * quads + (FT if down else 0)
        at["u"] += quads // 2 + (1 if down else 0)
        at["r"] += rounds + (1 if down else 0)
        at["rf"] += rounds

    stage("vec", rounds=1)
    stage("mem_norm", rounds=2)
    for l in range(LAYERS):
        stage(f"mk{l}", quads=4, rounds=2)
        stage(f"mv{l}", quads=4)
    for l in range(LAYERS):
        stage(f"pre_mix{l}", rounds=2)
        if l == 0:
            stage("sb_qk", quads=4, rounds=2)
            stage("sb_z", rounds=1)
            stage("sb_vu", quads=4)
            stage("sb_sum", rounds=1)
            stage("sb_pv", rounds=1)
            stage("pool_mean", rounds=1)
            stage("pool_map", rounds=1)
        else:
            stage("gla_qk", quads=4, rounds=2)
            stage("gla_a", rounds=1)
            stage("gla_at", rounds=1)
            stage("gla_g", rounds=1)
            stage("gla_v", quads=4)
            stage("gla_s", rounds=1)
            stage("gla_r", quads=4)
            stage("gla_o", rounds=GH // 2)
            stage("gla_t", rounds=2)
        stage(f"mix_out{l}", quads=4)
        stage(f"pre_x{l}", rounds=2)
        stage(f"xq{l}", quads=4, rounds=2)
        stage(f"x_s{l}", rounds=1)
        stage(f"x_pt{l}", rounds=1)
        stage(f"x_pv{l}", rounds=2)
        stage(f"x_out{l}", quads=4)
        stage(f"pre_ff{l}", rounds=2)
        stage(f"gu{l}", quads=2 * FF // NB, rounds=FF // NB)
        stage(f"down{l}", down=True)
    CHUNKS = at["c"]
    NORMS = ["mem_norm"] + [f"{n}{l}" for l in range(LAYERS) for n in ("pre_mix", "pre_x", "pre_ff")]
    POSTS = [f"{n}{l}" for l in range(LAYERS) for n in ("mix_out", "x_out", "down")]

    def cut(w, s):
        return w.rearrange("(s k p) n -> s p k n", s=4, p=P)[s]

    with ExitStack() as ctx:
        cursor = [(nc.sbuf_base + 31) // 32 * 32]

        def place(name, shape, dt, offset):
            return nc.alloc_sbuf_tensor_at(name, [P] + shape, dt, offset=offset)

        def sb(name, shape, dt=F32):
            size = 4
            for n in shape:
                size *= n
            t = place(name, shape, dt, cursor[0])
            cursor[0] += (size + 31) // 32 * 32
            return t

        def sem(name):
            return ctx.enter_context(nc.semaphore(name))

        KB = 1024
        w_raw = sb("w_raw", [RAW_SLOTS, CHUNK])
        w_hi = sb("w_hi", [W_SLOTS, CHUNK], F32R)
        w_lo = sb("w_lo", [W_SLOTS, CHUNK], F32R)
        xres = sb("xres", [MT, D])
        act_hi = sb("act_hi", [KT, T], F32R)
        act_lo = sb("act_lo", [KT, T], F32R)
        gain_at = cursor[0]
        gain = sb("gain", [D])
        stage_at = cursor[0]
        nat = sb("nat", [2, MT, NB])
        area = cursor[0]
        cursor[0] += 56 * KB
        gate_w_sb = place("gate_w_sb", [GH * GK], F32, gain_at)
        gnorm_sb = place("gnorm_sb", [GV], F32, gain_at + 4 * KB)
        a_t = place("a_t", [T], F32, gain_at + 6 * KB)
        gw_raw = place("gw_raw", [KT, RANK], F32, gain_at + 7 * KB)
        gla_e = place("gla_e", [8, NCH, CH], F32, stage_at)
        gla_sc = place("gla_sc", [GH, MT, T], F32, stage_at)
        memx = place("memx", [MT, D], F32, area + 16 * KB)
        y = place("y", [MT, D], F32, area)
        kx = place("kx", [KT, T], F32, area + 16 * KB)
        vx = place("vx", [MT, D], F32, area + 32 * KB)
        qx = place("qx", [KT, T], F32, area)
        px = place("px", [XH, MT, T], F32, area + 48 * KB)
        pxt = px
        qk = place("qk", [KT, T], F32, area)
        vu = place("vu", [MT, D], F32, area + 16 * KB)
        zs = place("zs", [SBH, 384], F32, area + 32 * KB)
        sp_t = place("sp_t", [SBH, 384], F32, area + 38 * KB)
        band = place("band", [4, MT, T], F32, area + 44 * KB)
        pooled = place("pooled", [8, T], F32, area)
        pw = place("pw", [4, 2, 256], F32, area + 8 * KB)
        gv = place("gv", [MT, D], F32, area + 16 * KB)
        gr = place("gr", [MT, D], F32, area + 32 * KB)
        qi = place("qi", [8, NCH, CH], F32, area + 32 * KB)
        ki = place("ki", [8, NCH, CH], F32, area + 40 * KB)
        gb = place("gb", [8, NCH, CH], F32, area + 48 * KB)
        qd = place("qd", [3, 8, CH], F32, area + 48 * KB)
        gate_u = place("gate_u", [8, T], F32, area + 32 * KB)
        mid = place("mid", [FT, T], F32, area)
        ident = sb("ident", [P])
        tri = sb("tri", [P])
        ones = sb("ones", [P])
        vec_rows = sb("vec_rows", [P])
        vec = sb("vec", [16])
        gw_hi = sb("gw_hi", [KT, RANK], F32R)
        gw_lo = sb("gw_lo", [KT, RANK], F32R)
        a_nat = sb("a_nat", [MT, RANK])
        ssq_part = sb("ssq_part", [MT, 4])
        ssq = sb("ssq", [MT])
        var = sb("var", [MT])
        rstd = sb("rstd", [MT])
        half = sb("half", [8])
        xmax = sb("xmax", [XH, MT])
        xden = sb("xden", [XH, MT])
        xrec = sb("xrec", [XH, MT])
        dec = sb("dec", [8, NCH])
        dec3 = sb("dec3", [8])
        ossq = sb("ossq", [8])
        ovar = sb("ovar", [8])
        orstd = sb("orstd", [8])
        scan_m = sb("scan_m", [NCH, CH])
        assert cursor[0] <= nc.sbuf_usable_end, (cursor[0], nc.sbuf_usable_end)

        ps = ctx.enter_context(nc.psum_tensor("ps", [P, 8, NB], F32))
        kv_dram = nc.dram_tensor("kv_scratch", (LAYERS, 2, P, KT * T), F32, kind="Internal").ap()

        raw_full = [sem(f"raw_full{i}") for i in range(RAW_SLOTS)]
        raw_claimed = sem("raw_claimed")
        hi_done = sem("hi_done")
        lo_done = sem("lo_done")
        w_used = sem("w_used")
        m0_done = sem("m0_done")
        bank_free = [sem(f"bank_free{i}") for i in range(8)]
        work_full = [None] * WORK + [sem(f"work_full{i}") for i in range(WORK, 8)]
        x_in = sem("x_in")
        mem_in = sem("mem_in")
        gain_in = sem("gain_in")
        kv_out = [sem(f"kv_out{i}") for i in range(2 * LAYERS)]
        kv_in = sem("kv_in")
        small_in = sem("small_in")
        gla_in = sem("gla_in")
        pw_in = sem("pw_in")
        y_out = sem("y_out")
        consts_done = sem("consts_done")
        vec_done = sem("vec_done")
        sq_done = sem("sq_done")
        y_scaled = sem("y_scaled")
        var_done = sem("var_done")
        rstd_done = sem("rstd_done")
        h_done = sem("h_done")
        x_done = sem("x_done")
        hi_ev = sem("hi_ev")
        jit_hi = sem("jit_hi")
        jit_done = sem("jit_done")
        z_done = sem("z_done")
        z_masked = sem("z_masked")
        l_done = sem("l_done")
        sp_done = sem("sp_done")
        w_log = sem("w_log")
        w_done = sem("w_done")
        pooled_hi = sem("pooled_hi")
        max_done = sem("max_done")
        exp_done = sem("exp_done")
        p_done = sem("p_done")
        g_done = sem("g_done")
        gate_done = sem("gate_done")
        e_done = sem("e_done")
        e_used = sem("e_used")
        sc_raw = sem("sc_raw")
        sc_done = sem("sc_done")
        osq_done = sem("osq_done")
        oroot_done = sem("oroot_done")
        gnorm_used = sem("gnorm_used")
        o_copied = sem("o_copied")
        o_done = sem("o_done")
        gw_done = sem("gw_done")
        band_done = sem("band_done")
        act_step = sem("act_step")
        dve_step = sem("dve_step")
        pool_step = sem("pool_step")

        def stepper(eng, s):
            n = [0]

            def then(ins):
                n[0] += 1
                ins.then_inc(s, 1)
                eng.wait_ge(s, n[0])
            return then

        hi_ev_at, n_ev = {}, 0
        for name, banks in ([("mem_norm", 8), ("pre_mix0", 8), ("sb_pv", 4), ("pool_map", 8), ("pre_x0", 8),
                             ("x_pv0", 8), ("pre_ff0", 8), ("pre_mix1", 8), ("gla_t", 8), ("pre_x1", 8),
                             ("x_pv1", 8), ("pre_ff1", 8)]):
            hi_ev_at[name] = n_ev
            n_ev += banks

        block = ctx.enter_context(nc.Block())

        @block.sync
        def _(sp):
            sp.sem_inc(lo_done, RAW_SLOTS)

            def load(src, c, s):
                sp.wait_ge(lo_done, c + s + 1)
                sp.sem_inc(raw_claimed, 1)
                dst = w_raw[:, s % RAW_SLOTS, :]
                if len(src.shape) == 3:
                    dst = dst.rearrange("p (k n) -> p k n", k=4)
                sp.dma_start(dst, src).then_inc(raw_full[s % RAW_SLOTS], 16)

            def pairs(name, w, n, col0=0):
                c0 = plan[name]["c"]
                with sp.Fori(0, n) as i:
                    for q in range(2):
                        for s in range(4):
                            src = cut(w, s)[:, :, bass.ds(i * (2 * NB) + (col0 + q * NB), NB)]
                            load(src, i * 8 + c0, 4 * q + s)

            for l in range(LAYERS):
                pairs(f"mk{l}", wk[l], 2)
                pairs(f"mv{l}", wv[l], 2)
            for l in range(LAYERS):
                if l == 0:
                    pairs("sb_qk", even_w_in, 2)
                    pairs("sb_vu", even_w_in, 2, 2 * SBW)
                    pairs("mix_out0", even_w_out, 2)
                else:
                    pairs("gla_qk", odd_w_in, 2)
                    pairs("gla_v", odd_w_in, 2, 2 * GH * GK)
                    pairs("gla_r", odd_w_in, 2, 2 * GH * GK + GH * GV)
                    pairs("mix_out1", odd_w_out, 2)
                pairs(f"xq{l}", wq[l], 2)
                pairs(f"x_out{l}", wo[l], 2)
                c0 = plan[f"gu{l}"]["c"]
                with sp.Fori(0, FF // NB) as i:
                    for q, w in enumerate((w_gate[l], w_up[l])):
                        for s in range(4):
                            load(cut(w, s)[:, :, bass.ds(i * NB, NB)], i * 8 + c0, 4 * q + s)
                c0 = plan[f"down{l}"]["c"]
                wd = w_down[l].rearrange("(i s p) n -> s p i n", s=4, p=P)
                with sp.Fori(0, FT // 4) as i:
                    for s in range(4):
                        load(wd[s][:, bass.ds(i, 1), :].rearrange("p o n -> p (o n)"), i * 4 + c0, s)
            for m in range(MT):
                sp.wait_ge(x_done, 2 * len(POSTS) - 1 + m)
                sp.dma_start(out[m * P:(m + 1) * P, :], xres[:, m, :]).then_inc(y_out, 16)
            sp.wait_ge(y_out, 16 * MT)

        @block.gpsimd
        def _(pool):
            then = stepper(pool, pool_step)

            def load_gain(k, row):
                pool.dma_start(gain[:], row.partition_broadcast(P)).then_inc(gain_in, 16)

            load_gain(0, mem_norm)
            then(nc.gpsimd.memset(ident[:], 0.0))
            nc.gpsimd.affine_select(out=ident[:], in_=ident[:], compare_op=ALU.not_equal, fill=1.0, base=0,
                                    pattern=[[-1, P]], channel_multiplier=1).then_inc(consts_done, 1)
            nc.gpsimd.memset(half[:], -0.5).then_inc(consts_done, 1)
            nc.gpsimd.memset(ones[:], 1.0).then_inc(consts_done, 1)
            pool.wait_ge(consts_done, 3)
            nc.gpsimd.affine_select(out=tri[:], in_=ones[:], compare_op=ALU.is_ge, fill=0.0, base=0,
                                    pattern=[[-1, P]], channel_multiplier=1).then_inc(consts_done, 1)
            then(nc.gpsimd.memset(scan_m[:], 1.0))
            then(nc.gpsimd.memset(scan_m[:, :, 0:1], 0.0))

            def rsqrt(k):
                pool.wait_ge(var_done, k + 1)
                nc.gpsimd.tensor_tensor(rstd[:], var[:], half[:, 0:MT], ALU.pow).then_inc(rstd_done, 1)

            n = [0]

            def norm_root():
                rsqrt(n[0])
                n[0] += 1

            def pre(k, nxt):
                norm_root()
                if nxt is not None:
                    pool.wait_ge(h_done, 2 * k + 2)
                    load_gain(None, nxt)

            def post(name, nxt):
                pl = plan[name]
                if name.startswith("down"):
                    pool.wait_ge(bank_free[7], pl["r"] + 2)
                else:
                    pool.wait_ge(bank_free[3], pl["u"] + 3)
                norm_root()
                if nxt is not None:
                    load_gain(None, nxt)

            pre(0, norms[0, 0])
            pre(1, norms[0, 1])
            for s_kv in kv_out:
                pool.wait_ge(s_kv, 16)
            for g in range(4):
                nc.gpsimd.memset(band[:, g, :, :], 1.0 / (2 << g)).then_inc(pool_step, 1)
            pool.wait_ge(pool_step, 3 + 4)
            for t in range((2 << 3) - 1):
                g0 = [g for g in range(4) if (2 << g) > t + 1][0]
                nc.gpsimd.memset(band[:, g0:4, :, t:t + 1], 1.0 / (t + 1)).then_inc(pool_step, 1)
            base = 3 + 4 + (2 << 3) - 1
            pool.wait_ge(pool_step, base)
            nc.gpsimd.affine_select(out=band[:], in_=band[:], compare_op=ALU.is_ge, fill=0.0, base=0,
                                    pattern=[[0, 4], [-P, MT], [1, T]], channel_multiplier=-1)\
                .then_inc(pool_step, 1)
            pool.wait_ge(pool_step, base + 1)
            for g in range(4):
                nc.gpsimd.affine_select(out=band[:, g, :, :], in_=band[:, g, :, :], compare_op=ALU.is_ge,
                                        fill=0.0, base=(2 << g) - 1, pattern=[[P, MT], [-1, T]],
                                        channel_multiplier=1).then_inc(consts_done, 1)
            for part, n_q in ((slice(0, T), T), (slice(T, 384), P)):
                pool.wait_ge(z_done, SBH)
                nc.gpsimd.affine_select(out=zs[:, :, part], in_=zs[:, :, part], compare_op=ALU.is_gt,
                                        fill=MASKED, base=0, pattern=[[0, SBH], [1, n_q]],
                                        channel_multiplier=-1).then_inc(z_masked, 1)
            pool.wait_ge(z_done, SBH)
            for g in range(4):
                pool.dma_start(pw[:, g, :, :], pool_w[g].rearrange("(k p) n -> p k n", p=P))\
                    .then_inc(pw_in, 16)
            for l in range(LAYERS):
                k = 1 + 3 * l
                if l == 1:
                    pool.wait_ge(sc_raw, 2 * GH)
                    for t, q0 in ((0, 0), (1, P)):
                        part = gla_sc[:, :, t, q0:T]
                        nc.gpsimd.affine_select(out=part, in_=part, compare_op=ALU.is_ge, fill=0.0, base=0,
                                                pattern=[[0, GH], [1, T - q0]], channel_multiplier=-1)\
                            .then_inc(sc_done, 1)
                    pool.wait_ge(osq_done, 1)
                    nc.gpsimd.tensor_tensor(orstd[:], ovar[:], half[:], ALU.pow).then_inc(oroot_done, 1)
                    pool.wait_ge(gnorm_used, 1)
                    load_gain(None, norms[1, 1])
                core = plan["pool_map"] if l == 0 else plan["gla_t"]
                pool.wait_ge(bank_free[7], core["r"] + (2 if l == 0 else 3))
                for s_kv in kv_out:
                    pool.wait_ge(s_kv, 16)
                pool.dma_start(kx[:].rearrange("p k t -> p (k t)"), kv_dram[l, 0]).then_inc(kv_in, 16)
                pool.dma_start(vx[:].rearrange("p m n -> p (m n)"), kv_dram[l, 1]).then_inc(kv_in, 16)
                post(f"mix_out{l}", norms[l, 2])
                pre(k + 1, norms[l, 3])
                post(f"x_out{l}", norms[l, 4])
                pre(k + 2, norms[l, 5])
                post(f"down{l}", norms[1, 0] if l == 0 else None)
                if l == 0:
                    pre(4, None)
                    pool.wait_ge(h_done, 2 * 4 + 2)
                    pool.dma_start(gate_w_sb[0:RANK, :], gate_w).then_inc(gla_in, 16)
                    pool.dma_start(gnorm_sb[:], gnorm.partition_broadcast(P)).then_inc(gla_in, 16)
                    pool.dma_start(gw_raw[:], odd_w_in[:, 2 * GH * (GK + GV):].rearrange(
                        "(k p) n -> p k n", p=P)).then_inc(gla_in, 16)

        @block.scalar
        def _(act):
            then = stepper(act, act_step)
            act.dma_start(memx[:], mem.rearrange("(m p) n -> p m n", p=P)).then_inc(mem_in, 16)
            act.dma_start(vec_rows[0:8, :], pool_scale.rearrange("(k p) -> k p", p=P)).then_inc(small_in, 16)
            act.dma_start(vec_rows[8:16, :], gate_b.rearrange("(k p) -> k p", p=P)).then_inc(small_in, 16)
            act.dma_start(xres[:], x.rearrange("(m p) n -> p m n", p=P)).then_inc(x_in, 16)

            def split(c, s):
                act.wait_ge(raw_full[s % RAW_SLOTS], c * 8 + (16 * (s // RAW_SLOTS) + 16))
                act.wait_ge(w_used, c + (s + 1))
                nc.scalar.activation(w_hi[:, s % W_SLOTS, :], w_raw[:, s % RAW_SLOTS, :], ACT.Copy)\
                    .then_inc(hi_done, 1)

            def norm(name):
                k = NORMS.index(name)
                src = memx if k == 0 else xres
                for m in range(MT):
                    if k == 0:
                        act.wait_ge(mem_in, 16)
                    elif k == 1:
                        act.wait_ge(x_in, 16)
                        act.wait_ge(work_full[7], plan["mem_norm"]["rf"] + 2)
                    else:
                        act.wait_ge(x_done, 2 * (k - 2) + m + 1)
                    nc.scalar.activation(y[:, m, :], src[:, m, :], ACT.Square, accum_out=ssq[:, m:m + 1])\
                        .then_inc(sq_done, 1)

            def round_transposes(name):
                pl = plan[name]
                for m in range(MT):
                    for b in range(4):
                        act.wait_ge(work_full[WORK + b], pl["rf"] + m + 1)
                        nc.scalar.activation(
                            act_hi[:, 4 * b:4 * b + 4, m * P:(m + 1) * P],
                            ps[:, WORK + b, :].rearrange("p (k t) -> p k t", t=P), ACT.Copy).then_inc(hi_ev, 1)

            def pair(c, evac0, mid_pair, evac1, end_pair, more=True):
                for s in range(4, 7):
                    split(c, s)
                evac0()
                split(c, 7)
                if more:
                    split(c, 8)
                mid_pair()
                if more:
                    split(c, 9)
                    split(c, 10)
                evac1()
                if more:
                    split(c, 11)
                end_pair()

            nothing = lambda: None

            def take_m0(i, pl, q, dst, func=ACT.Copy, reuse=None):
                def run():
                    act.wait_ge(m0_done, i * 2 + (pl["a"] + q + 1))
                    if reuse is not None:
                        act.wait_ge(*reuse)
                    nc.scalar.activation(dst, ps[:, 2 * q, :], func).then_inc(bank_free[2 * q], 1)
                return run

            def transposed(name, dst, tile0=0):
                pl = plan[name]
                with act.Fori(0, 2) as i:
                    def take_t(q):
                        def run():
                            b = WORK + 2 * q
                            act.wait_ge(work_full[b], i + (pl["rf"] + 1))
                            nc.scalar.activation(dst[:, bass.ds(i * 8 + (tile0 + 4 * q), 2), :],
                                                 ps[:, b, :].rearrange("p (k t) -> p k t", t=T), ACT.Copy)\
                                .then_inc(bank_free[b], 1)
                        return run

                    def reuse(q):
                        return (work_full[WORK + 2 * q + 1], i + pl["rf"]) if pl["rf"] else None
                    pair(i * 8 + pl["c"],
                         take_m0(i, pl, 0, nat[:, 0, 0, :], reuse=reuse(0)), take_t(0),
                         take_m0(i, pl, 1, nat[:, 1, 0, :], reuse=reuse(1)), take_t(1))

            def natural(name, dst, func=ACT.Copy):
                pl = plan[name]
                with act.Fori(0, 2) as i:
                    pair(i * 8 + pl["c"],
                         take_m0(i, pl, 0, dst[:, 0, bass.ds(i * (2 * NB), NB)], func), nothing,
                         take_m0(i, pl, 1, dst[:, 0, bass.ds(i * (2 * NB) + NB, NB)], func), nothing)

            banks_squared = [0]

            def square_y(name):
                pl = plan[name]
                y0 = banks_squared[0]
                with act.Fori(0, 2) as i:
                    def squares(q):
                        def run():
                            for m in range(MT):
                                act.wait_ge(y_scaled, i * 4 + (y0 + 2 * q + m + 1))
                                bank = ps[:, 2 * q + m, :]
                                nc.scalar.activation(bank, bank, ACT.Square,
                                                     accum_out=ssq_part[:, m, bass.ds(i * 2 + q, 1)])\
                                    .then_inc(bank_free[2 * q + m], 1)
                        return run
                    pair(i * 8 + pl["c"], squares(0), nothing, squares(1), nothing)
                banks_squared[0] += 8

            def round_tiles(name, banks, first_tile, n_tiles, scale=None):
                pl = plan[name]
                for k, (b, rnd) in enumerate(banks):
                    act.wait_ge(work_full[b], pl["rf"] + rnd + 1)
                    if scale is None:
                        nc.scalar.activation(act_hi[:, first_tile + 2 * k:first_tile + 2 * k + 2, :],
                                             ps[:, b, :].rearrange("p (k t) -> p k t", t=T), ACT.Copy)\
                            .then_inc(hi_ev, 1)
                    else:
                        for j in range(2):
                            t = 2 * k + j
                            nc.scalar.activation(act_hi[:, first_tile + t, :], ps[:, b, j * T:(j + 1) * T],
                                                 ACT.Copy, scale=scale[:, t:t + 1]).then_inc(hi_ev, 1)

            norm("mem_norm")
            round_transposes("mem_norm")
            for s in range(W_SLOTS):
                split(0, s)
            for l in range(LAYERS):
                if l:
                    act.wait_ge(kv_out[2 * l - 2], 16)
                transposed(f"mk{l}", kx)
                pl = plan[f"mk{l}"]
                for b in range(WORK, 8):
                    act.wait_ge(bank_free[b], pl["r"] + 3)
                act.dma_start(kv_dram[l, 0], kx[:].rearrange("p k t -> p (k t)")).then_inc(kv_out[2 * l], 16)
                if l:
                    act.wait_ge(kv_out[2 * l - 1], 16)
                natural(f"mv{l}", vx)
                pl = plan[f"mv{l}"]
                for b in range(4):
                    act.wait_ge(bank_free[b], pl["u"] + 3)
                act.dma_start(kv_dram[l, 1], vx[:].rearrange("p m n -> p (m n)")).then_inc(kv_out[2 * l + 1], 16)

            for l in range(LAYERS):
                norm(f"pre_mix{l}")
                round_transposes(f"pre_mix{l}")
                if l == 0:
                    transposed("sb_qk", qk)
                    pl = plan["sb_z"]
                    for s_kv in kv_out:
                        act.wait_ge(s_kv, 16)
                    for h in range(SBH):
                        act.wait_ge(work_full[WORK + h], pl["rf"] + 1)
                        nc.scalar.activation(zs[:, h, :], ps[:, WORK + h, 0:384], ACT.Copy, scale=SBD ** -0.5)\
                            .then_inc(z_done, 1)
                        act.wait_ge(z_done, h + 1)
                        act.sem_inc(bank_free[WORK + h], 1)
                    act.wait_ge(z_masked, 2)
                    then(nc.scalar.activation(sp_t[:], zs[:], ACT.Abs))
                    then(nc.scalar.activation(sp_t[:], sp_t[:], ACT.Exp, scale=-1.0))
                    nc.scalar.activation(sp_t[:], sp_t[:], ACT.Ln, bias=1.0).then_inc(l_done, 1)
                    natural("sb_vu", vu)
                    act.wait_ge(w_log, SBH)
                    nc.scalar.activation(zs[:], zs[:], ACT.Exp).then_inc(w_done, 1)
                    round_tiles("sb_pv", [(WORK + h, 0) for h in range(SBH)], 0, 8)
                    pl = plan["pool_mean"]
                    for b in (4, 6):
                        act.wait_ge(work_full[b], pl["rf"] + 1)
                        nc.scalar.activation(pooled[:, 2 * (b - WORK):2 * (b - WORK) + 2, :],
                                             ps[:, b, :].rearrange("p (k t) -> p k t", t=T), ACT.Copy)\
                            .then_inc(bank_free[b], 1)
                    act.wait_ge(vec_done, 1)
                    round_tiles("pool_map", [(WORK + g, 0) for g in range(4)], 8, 8, scale=vec[:, 0:8])
                else:
                    transposed("gla_qk", qk)
                    act.wait_ge(gla_in, 16 * 3)
                    nc.scalar.activation(gw_hi[:], gw_raw[:], ACT.Copy).then_inc(gw_done, 1)
                    pl = plan["gla_g"]
                    for t in range(8):
                        b, j = WORK + t // 2, t % 2
                        act.wait_ge(work_full[b], pl["rf"] + 1)
                        nc.scalar.activation(gb[:, t, :, :].rearrange("p c t -> p (c t)"),
                                             ps[:, b, j * T:(j + 1) * T], ACT.Abs, bias=vec[:, 8 + t:9 + t])\
                            .then_inc(g_done, 1)
                    act.wait_ge(g_done, 8)
                    then(nc.scalar.activation(gb[:], gb[:], ACT.Exp, scale=-1.0))
                    nc.scalar.activation(gb[:], gb[:], ACT.Ln, bias=1.0).then_inc(g_done, 1)
                    s16 = 1.0 / 16.0
                    act.wait_ge(gate_done, 1)
                    then(nc.scalar.activation(qi[:], gla_e[:], ACT.Exp, scale=s16))
                    nc.scalar.activation(ki[:], gla_e[:], ACT.Exp, scale=-s16).then_inc(e_done, 1)
                    act.wait_ge(e_used, 1)
                    nc.scalar.activation(gla_e[:], gla_e[:], ACT.Exp, scale=s16).then_inc(e_done, 1)
                    nc.scalar.activation(dec[:], gb[:, :, :, CH - 1], ACT.Exp, scale=s16).then_inc(e_done, 1)
                    act.wait_ge(e_used, 2)
                    nc.scalar.activation(gla_e[:], gb[:], ACT.Exp, scale=s16).then_inc(e_done, 1)
                    natural("gla_v", gv)
                    pl = plan["gla_s"]
                    act.wait_ge(e_used, 3)
                    for h in range(GH):
                        act.wait_ge(work_full[WORK + h], pl["rf"] + 1)
                        nc.scalar.activation(gla_sc[:, h, 0, :], ps[:, WORK + h, 0:T], ACT.Copy)\
                            .then_inc(sc_raw, 1)
                        nc.scalar.activation(gla_sc[:, h, 1, P:T], ps[:, WORK + h, T + P:2 * T], ACT.Copy)\
                            .then_inc(sc_raw, 1)
                        act.wait_ge(sc_raw, 2 * h + 2)
                        act.sem_inc(bank_free[WORK + h], 1)
                    pl = plan["gla_r"]
                    with act.Fori(0, 2) as i:
                        def silu_r(q):
                            def run():
                                for m in range(MT):
                                    if m == 0:
                                        act.wait_ge(m0_done, i * 2 + (pl["a"] + q + 1))
                                    else:
                                        act.wait_ge(w_used, i * 8 + (pl["c"] + 4 * q + 4 + W_SLOTS))
                                    nc.scalar.activation(gr[:, m, bass.ds(i * (2 * NB) + q * NB, NB)],
                                                         ps[:, 2 * q + m, :], ACT.Silu)\
                                        .then_inc(bank_free[2 * q + m], 1)
                            return run
                        pair(i * 8 + pl["c"], silu_r(0), nothing, silu_r(1), nothing)
                    pl = plan["gla_o"]
                    for h in range(GH):
                        for m in range(MT):
                            b = WORK + 2 * (h % 2) + m
                            act.wait_ge(o_copied, 2 * h + m + 1)
                            nc.scalar.activation(ps[:, b, :], ps[:, b, :], ACT.Square,
                                                 accum_out=ossq[:, 2 * h + m:2 * h + m + 1])\
                                .then_inc(bank_free[b], 1)
                    round_transposes("gla_t")
                square_y(f"mix_out{l}")
                norm(f"pre_x{l}")
                round_transposes(f"pre_x{l}")
                transposed(f"xq{l}", qx)
                for h in range(XH):
                    for m in range(MT):
                        k = (l * XH + h) * MT + m
                        act.wait_ge(max_done, k + 1)
                        nc.scalar.activation(px[:, h, m, :], ps[:, WORK + h, m * T:(m + 1) * T], ACT.Exp,
                                             bias=xmax[:, h, m:m + 1], scale=XD ** -0.5,
                                             accum_out=xden[:, h, m:m + 1]).then_inc(exp_done, 1)
                    act.wait_ge(exp_done, (l * XH + h) * MT + 2)
                    act.sem_inc(bank_free[WORK + h], 1)
                pl = plan[f"x_pt{l}"]
                for b in (4, 6):
                    act.wait_ge(work_full[7], pl["rf"] + 1)
                    act.wait_ge(work_full[b], pl["rf"] + 1)
                    nc.scalar.activation(pxt[:, b - WORK, :, :],
                                         ps[:, b, :].rearrange("p (k t) -> p k t", t=T), ACT.Copy)\
                        .then_inc(bank_free[b], 1)
                round_tiles(f"x_pv{l}", [(WORK + k % 4, k // 4) for k in range(8)], 0, 16)
                square_y(f"x_out{l}")
                norm(f"pre_ff{l}")
                round_transposes(f"pre_ff{l}")
                pl = plan[f"gu{l}"]
                with act.Fori(0, FF // NB) as i:
                    def silu():
                        for m in range(MT):
                            if m == 0:
                                act.wait_ge(m0_done, i * 2 + (pl["a"] + 1))
                            else:
                                act.wait_ge(w_used, i * 8 + (pl["c"] + 4 + W_SLOTS))
                            act.wait_ge(bank_free[2 + m], i + (pl["u"] + 1))
                            nc.scalar.activation(nat[:, 1, m, :], ps[:, m, :], ACT.Silu)\
                                .then_inc(bank_free[m], 1)

                    def take_mid():
                        for b in (4, 6):
                            act.wait_ge(work_full[b], i + (pl["rf"] + 1))
                            nc.scalar.activation(mid[:, bass.ds(i * 4 + (b - WORK), 1), :], ps[:, b:b + 1, 0:T],
                                                 ACT.Copy).then_inc(bank_free[b], 1)
                    pair(i * 8 + pl["c"], silu, nothing, nothing, take_mid)
                pu, pl = pl, plan[f"down{l}"]
                jit0 = l * FT
                for b in range(WORK, 8):
                    act.wait_ge(bank_free[b], pl["r"] + 1)

                def jit(i, s):
                    act.wait_ge(w_used, i * 4 + (pl["c"] + s - 4 + 1 + W_SLOTS))
                    nc.scalar.activation(act_hi[:, s % 4:s % 4 + 1, :], mid[:, bass.ds(i * 4 + s, 1), :],
                                         ACT.Copy).then_inc(jit_hi, 1)
                act.wait_ge(w_used, pl["c"] + W_SLOTS)
                for s in range(4):
                    nc.scalar.activation(act_hi[:, s, :], mid[:, s, :], ACT.Copy).then_inc(jit_hi, 1)
                with act.Fori(0, FT // 4 - 1) as i:
                    for s in range(4):
                        jit(i, s + 4)
                        split(i * 4 + pl["c"], s + 4)
                if l < LAYERS - 1:
                    for s in range(4):
                        split(pl["c"] + FT - 4, s + 4)
                for m in range(MT):
                    for n in range(4):
                        act.wait_ge(y_scaled, banks_squared[0] + 4 * m + n + 1)
                        bank = ps[:, 4 * m + n, :]
                        nc.scalar.activation(bank, bank, ACT.Square, accum_out=ssq_part[:, m, n:n + 1])\
                            .then_inc(bank_free[4 * m + n], 1)
                banks_squared[0] += 8

        @block.vector
        def _(dve):
            then = stepper(dve, dve_step)

            def split(c, s):
                dve.wait_ge(hi_done, c + (s + 1))
                nc.vector.tensor_tensor(w_lo[:, s % W_SLOTS, :], w_raw[:, s % RAW_SLOTS, :],
                                        w_hi[:, s % W_SLOTS, :].bitcast(F32), ALU.subtract)\
                    .then_inc(lo_done, 1)

            roots = [0]

            def root(src):
                nc.vector.tensor_scalar(var[:], src, 1.0 / D, EPS, ALU.mult, ALU.add).then_inc(var_done, 1)
                roots[0] += 1
                dve.wait_ge(rstd_done, roots[0])

            gains = [0]

            def gain_ready():
                gains[0] += 1
                dve.wait_ge(gain_in, 16 * gains[0])

            def norm(name):
                k = NORMS.index(name)
                src = memx if k == 0 else xres
                dve.wait_ge(sq_done, 2 * k + 2)
                root(ssq[:])
                gain_ready()
                for m in range(MT):
                    nc.vector.scalar_tensor_tensor(out=y[:, m, :], in0=src[:, m, :], scalar=rstd[:, m:m + 1],
                                                   in1=gain[:], op0=ALU.mult, op1=ALU.mult)\
                        .then_inc(h_done, 1)

            def rest_transposes(name):
                e0 = hi_ev_at[name]
                for m in range(MT):
                    for b in range(4):
                        dve.wait_ge(hi_ev, e0 + 4 * m + b + 1)
                        sl = (slice(None), slice(4 * b, 4 * b + 4), slice(m * P, (m + 1) * P))
                        nc.vector.tensor_tensor(act_lo[sl], ps[:, WORK + b, :].rearrange("p (k t) -> p k t", t=P),
                                                act_hi[sl].bitcast(F32), ALU.subtract)\
                            .then_inc(bank_free[WORK + b], 1)

            def pair(c, evac0, mid_pair, evac1, end_pair):
                for s in range(4, 7):
                    split(c, s)
                evac0()
                split(c, 7)
                split(c, 8)
                mid_pair()
                split(c, 9)
                split(c, 10)
                evac1()
                split(c, 11)
                end_pair()

            nothing = lambda: None

            def take_m1(i, pl, q, dst, reuse=None):
                def run():
                    dve.wait_ge(w_used, i * 8 + (pl["c"] + 4 * q + 4 + W_SLOTS))
                    if reuse is not None:
                        dve.wait_ge(*reuse)
                    nc.vector.tensor_copy(dst, ps[:, 2 * q + 1, :]).then_inc(bank_free[2 * q + 1], 1)
                return run

            def transposed(name, dst):
                pl = plan[name]
                with dve.Fori(0, 2) as i:
                    def take_t(q):
                        def run():
                            b = WORK + 2 * q + 1
                            dve.wait_ge(work_full[b], i + (pl["rf"] + 1))
                            nc.vector.tensor_copy(dst[:, bass.ds(i * 8 + (4 * q + 2), 2), :],
                                                  ps[:, b, :].rearrange("p (k t) -> p k t", t=T))\
                                .then_inc(bank_free[b], 1)
                        return run

                    def reuse(q):
                        return (work_full[WORK + 2 * q + 1], i + pl["rf"]) if pl["rf"] else None
                    pair(i * 8 + pl["c"],
                         take_m1(i, pl, 0, nat[:, 0, 1, :], reuse(0)), take_t(0),
                         take_m1(i, pl, 1, nat[:, 1, 1, :], reuse(1)), take_t(1))

            def natural(name, dst):
                pl = plan[name]
                with dve.Fori(0, 2) as i:
                    pair(i * 8 + pl["c"],
                         take_m1(i, pl, 0, dst[:, 1, bass.ds(i * (2 * NB), NB)]), nothing,
                         take_m1(i, pl, 1, dst[:, 1, bass.ds(i * (2 * NB) + NB, NB)]), nothing)

            def scale_y(name):
                pl = plan[name]
                gain_ready()
                with dve.Fori(0, 2) as i:
                    def scale(q):
                        def run():
                            for m in range(MT):
                                if m == 0:
                                    dve.wait_ge(m0_done, i * 2 + (pl["a"] + q + 1))
                                else:
                                    dve.wait_ge(w_used, i * 8 + (pl["c"] + 4 * q + 4 + W_SLOTS))
                                cols = bass.ds(i * (2 * NB) + q * NB, NB)
                                nc.vector.tensor_tensor(y[:, m, cols], ps[:, 2 * q + m, :], gain[:, cols],
                                                        ALU.mult).then_inc(y_scaled, 1)
                        return run
                    pair(i * 8 + pl["c"], scale(0), nothing, scale(1), nothing)

            def add_y(last_bank, last_count):
                dve.wait_ge(bank_free[last_bank], last_count)
                then(nc.vector.tensor_reduce(ssq[:], ssq_part[:], AX_X, ALU.add))
                root(ssq[:])
                for m in range(MT):
                    nc.vector.scalar_tensor_tensor(out=xres[:, m, :], in0=y[:, m, :], scalar=rstd[:, m:m + 1],
                                                   in1=xres[:, m, :], op0=ALU.mult, op1=ALU.add)\
                        .then_inc(x_done, 1)

            def rest_tiles(name, banks, first_tile, scale=None):
                e0 = hi_ev_at[name]
                for k, b in enumerate(banks):
                    if scale is None:
                        dve.wait_ge(hi_ev, e0 + k + 1)
                        sl = slice(first_tile + 2 * k, first_tile + 2 * k + 2)
                        nc.vector.tensor_tensor(act_lo[:, sl, :], ps[:, b, :].rearrange("p (k t) -> p k t", t=T),
                                                act_hi[:, sl, :].bitcast(F32), ALU.subtract)\
                            .then_inc(bank_free[b], 1)
                    else:
                        for j in range(2):
                            t = 2 * k + j
                            dve.wait_ge(hi_ev, e0 + 2 * k + 2)
                            ins = nc.vector.scalar_tensor_tensor(
                                out=act_lo[:, first_tile + t, :], in0=ps[:, b, j * T:(j + 1) * T],
                                scalar=scale[:, t:t + 1], in1=act_hi[:, first_tile + t, :].bitcast(F32),
                                op0=ALU.mult, op1=ALU.subtract)
                        ins.then_inc(bank_free[b], 1)

            dve.wait_ge(work_full[4], 1)
            nc.vector.tensor_copy(vec[:], ps[:, 4, 0:16]).then_inc(vec_done, 1)
            dve.wait_ge(vec_done, 1)
            dve.sem_inc(bank_free[4], 1)
            norm("mem_norm")
            rest_transposes("mem_norm")
            for s in range(W_SLOTS):
                split(0, s)
            for l in range(LAYERS):
                if l:
                    dve.wait_ge(kv_out[2 * l - 2], 16)
                transposed(f"mk{l}", kx)
                if l:
                    dve.wait_ge(kv_out[2 * l - 1], 16)
                natural(f"mv{l}", vx)

            for l in range(LAYERS):
                norm(f"pre_mix{l}")
                rest_transposes(f"pre_mix{l}")
                if l == 0:
                    transposed("sb_qk", qk)
                    dve.wait_ge(l_done, 1)
                    nc.vector.scalar_tensor_tensor(out=sp_t[:], in0=zs[:], scalar=0.0, in1=sp_t[:],
                                                   op0=ALU.max, op1=ALU.add).then_inc(sp_done, 1)
                    dve.wait_ge(consts_done, 8)
                    for k in range(MT):
                        nc.vector.tensor_tensor(band[:, :, k, k * P:(k + 1) * P], band[:, :, k, k * P:(k + 1) * P],
                                                ident[:].unsqueeze(1).broadcast_to([P, 4, P]), ALU.subtract)\
                            .then_inc(band_done, 1)
                    natural("sb_vu", vu)
                    pl = plan["sb_sum"]
                    for h in range(SBH):
                        dve.wait_ge(work_full[WORK + h], pl["rf"] + 1)
                        nc.vector.tensor_tensor(zs[:, h, :], zs[:, h, :], ps[:, WORK + h, 0:384], ALU.subtract)\
                            .then_inc(w_log, 1)
                        dve.wait_ge(w_log, h + 1)
                        dve.sem_inc(bank_free[WORK + h], 1)
                    rest_tiles("sb_pv", [WORK + h for h in range(SBH)], 0)
                    pl = plan["pool_mean"]
                    for b in (5, 7):
                        dve.wait_ge(work_full[b], pl["rf"] + 1)
                        nc.vector.tensor_copy(pooled[:, 2 * (b - WORK):2 * (b - WORK) + 2, :],
                                              ps[:, b, :].rearrange("p (k t) -> p k t", t=T))\
                            .then_inc(bank_free[b], 1)
                    rest_tiles("pool_map", [WORK + g for g in range(4)], 8, scale=vec[:, 0:8])
                else:
                    transposed("gla_qk", qk)
                    dve.wait_ge(gw_done, 1)
                    nc.vector.tensor_tensor(gw_lo[:], gw_raw[:], gw_hi[:].bitcast(F32), ALU.subtract)\
                        .then_inc(gw_done, 1)
                    for m in range(MT):
                        dve.wait_ge(work_full[WORK + m], plan["gla_a"]["rf"] + 1)
                        nc.vector.tensor_copy(a_nat[:, m, :], ps[:, WORK + m, 0:RANK])\
                            .then_inc(bank_free[WORK + m], 1)
                    dve.wait_ge(work_full[4], plan["gla_at"]["rf"] + 1)
                    nc.vector.tensor_copy(a_t[0:RANK, :], ps[0:RANK, 4, 0:T]).then_inc(bank_free[4], 1)
                    pl = plan["gla_g"]
                    dve.wait_ge(g_done, 8)
                    for t in range(8):
                        b, j = WORK + t // 2, t % 2
                        ins = nc.vector.tensor_scalar(gate_u[:, t, :], ps[:, b, j * T:(j + 1) * T],
                                                      vec[:, 8 + t:9 + t], 0.0, ALU.add, ALU.min)
                        if j:
                            ins.then_inc(bank_free[b], 1)
                    dve.wait_ge(bank_free[7], pl["r"] + 2)
                    dve.wait_ge(g_done, 9)
                    then(nc.vector.tensor_tensor(gate_u[:], gate_u[:], gb[:].rearrange("p k c t -> p k (c t)"),
                                                 ALU.subtract))
                    dve.wait_ge(pool_step, 3)
                    for t in range(8):
                        ins = nc.vector.tensor_tensor_scan(
                            gb[:, t, :, :].rearrange("p c t -> p (c t)"), scan_m[:].rearrange("p c t -> p (c t)"),
                            gate_u[:, t, :], 0.0, ALU.mult, ALU.add)
                        then(ins)
                    def fours(tns):
                        return tns[:].rearrange("p k c t -> p (k c) t")
                    bc = lambda col: fours(gb)[:, :, col:col + 1].broadcast_to([P, 8 * NCH, CH])
                    nc.vector.tensor_tensor(fours(gla_e), fours(gb), bc(CH // 2), ALU.subtract)\
                        .then_inc(gate_done, 1)
                    dve.wait_ge(e_done, 1)
                    nc.vector.tensor_tensor(fours(gla_e), bc(CH - 1), fours(gb), ALU.subtract)\
                        .then_inc(e_used, 1)
                    qt = qk[:, 0:8, :].rearrange("p k t -> p (k t)")
                    kt_ = qk[:, 8:16, :].rearrange("p k t -> p (k t)")
                    flat = lambda tns: tns[:].rearrange("p k c t -> p (k c t)")
                    nc.vector.scalar_tensor_tensor(out=flat(qi), in0=flat(qi), scalar=GK ** -0.5, in1=qt,
                                                   op0=ALU.mult, op1=ALU.mult)
                    nc.vector.tensor_tensor(flat(ki), flat(ki), kt_, ALU.mult)
                    dve.wait_ge(e_done, 3)
                    nc.vector.tensor_tensor(kt_, kt_, flat(gla_e), ALU.mult).then_inc(e_used, 1)
                    dve.wait_ge(e_done, 4)
                    then(nc.vector.scalar_tensor_tensor(out=qt, in0=flat(gla_e), scalar=GK ** -0.5, in1=qt,
                                                        op0=ALU.mult, op1=ALU.mult))
                    then(nc.vector.tensor_tensor(dec3[:].unsqueeze(2), dec[:, :, 1:2], dec[:, :, 2:3], ALU.mult))
                    q4 = qk[:, 0:8, :].rearrange("p k (c t) -> p k c t", t=CH)
                    for j, (cq, d) in enumerate(((2, dec[:, :, 1:2]), (3, dec[:, :, 2:3]), (3, dec3[:].unsqueeze(2)))):
                        ins = nc.vector.tensor_tensor(qd[:, j, :, :], q4[:, :, cq, :],
                                                      d.broadcast_to([P, 8, CH]), ALU.mult)
                    ins.then_inc(e_used, 1)
                    natural("gla_v", gv)
                    pl = plan["gla_r"]
                    with dve.Fori(0, 2) as i:
                        pair(i * 8 + pl["c"], nothing, nothing, nothing, nothing)
                    pl = plan["gla_o"]
                    for h in range(GH):
                        for m in range(MT):
                            b = WORK + 2 * (h % 2) + m
                            dve.wait_ge(work_full[b], pl["rf"] + h // 2 + 1)
                            nc.vector.tensor_copy(y[:, m, h * GV:(h + 1) * GV], ps[:, b, :])\
                                .then_inc(o_copied, 1)
                    for b in range(WORK, 8):
                        dve.wait_ge(bank_free[b], pl["r"] + 3)
                    nc.vector.tensor_scalar(ovar[:], ossq[:], 1.0 / GV, EPS, ALU.mult, ALU.add)\
                        .then_inc(osq_done, 1)
                    dve.wait_ge(oroot_done, 1)
                    dve.wait_ge(gla_in, 16 * 3)
                    for h in range(GH):
                        for m in range(MT):
                            cols = slice(h * GV, (h + 1) * GV)
                            ins = nc.vector.scalar_tensor_tensor(
                                out=y[:, m, cols], in0=y[:, m, cols], scalar=orstd[:, 2 * h + m:2 * h + m + 1],
                                in1=gnorm_sb[:], op0=ALU.mult, op1=ALU.mult)
                    ins.then_inc(gnorm_used, 1)
                    dve.wait_ge(gnorm_used, 1)
                    for b in range(4):
                        dve.wait_ge(bank_free[b], plan["gla_r"]["u"] + 3)
                    for m in range(MT):
                        nc.vector.tensor_tensor(y[:, m, :], y[:, m, :], gr[:, m, :], ALU.mult).then_inc(o_done, 1)
                    rest_transposes("gla_t")
                scale_y(f"mix_out{l}")
                add_y(3, plan[f"mix_out{l}"]["u"] + 3)
                norm(f"pre_x{l}")
                rest_transposes(f"pre_x{l}")
                transposed(f"xq{l}", qx)
                pl = plan[f"x_s{l}"]
                for h in range(XH):
                    dve.wait_ge(work_full[WORK + h], pl["rf"] + 1)
                    then(nc.vector.tensor_reduce(xden[:, h, :], ps[:, WORK + h, :].rearrange("p (m t) -> p m t", t=T),
                                                 AX_X, ALU.max))
                    nc.vector.tensor_scalar(xmax[:, h, :], xden[:, h, :], -XD ** -0.5, None, ALU.mult)\
                        .then_inc(max_done, MT)
                for h in range(XH):
                    dve.wait_ge(exp_done, (l * XH + h) * MT + 2)
                    then(nc.vector.reciprocal(xrec[:, h, :], xden[:, h, :]))
                    for m in range(MT):
                        nc.vector.tensor_scalar(px[:, h, m, :], px[:, h, m, :], xrec[:, h, m:m + 1], None,
                                                ALU.mult).then_inc(p_done, 1)
                pl = plan[f"x_pt{l}"]
                for b in (5, 7):
                    dve.wait_ge(work_full[7], pl["rf"] + 1)
                    nc.vector.tensor_copy(pxt[:, b - WORK, :, :],
                                          ps[:, b, :].rearrange("p (k t) -> p k t", t=T))\
                        .then_inc(bank_free[b], 1)
                rest_tiles(f"x_pv{l}", [WORK + k % 4 for k in range(8)], 0)
                scale_y(f"x_out{l}")
                add_y(3, plan[f"x_out{l}"]["u"] + 3)
                norm(f"pre_ff{l}")
                rest_transposes(f"pre_ff{l}")
                pl = plan[f"gu{l}"]
                with dve.Fori(0, FF // NB) as i:
                    def times_up():
                        for m in range(MT):
                            dve.wait_ge(bank_free[m], i + (pl["u"] + 2))
                            if m == 0:
                                dve.wait_ge(m0_done, i * 2 + (pl["a"] + 2))
                            else:
                                dve.wait_ge(w_used, i * 8 + (pl["c"] + 8 + W_SLOTS))
                            dve.wait_ge(work_full[7], i + pl["rf"])
                            nc.vector.tensor_tensor(nat[:, 0, m, :], ps[:, 2 + m, :], nat[:, 1, m, :], ALU.mult)\
                                .then_inc(bank_free[2 + m], 1)

                    def take_mid():
                        for b in (5, 7):
                            dve.wait_ge(work_full[b], i + (pl["rf"] + 1))
                            nc.vector.tensor_copy(mid[:, bass.ds(i * 4 + (b - WORK), 1), :], ps[:, b:b + 1, 0:T])\
                                .then_inc(bank_free[b], 1)
                    pair(i * 8 + pl["c"], nothing, nothing, times_up, take_mid)
                pl = plan[f"down{l}"]
                jit0 = l * FT

                def jit(i, s):
                    dve.wait_ge(jit_hi, i * 4 + (jit0 + s + 1))
                    nc.vector.tensor_tensor(act_lo[:, s % 4:s % 4 + 1, :], mid[:, bass.ds(i * 4 + s, 1), :],
                                            act_hi[:, s % 4:s % 4 + 1, :].bitcast(F32), ALU.subtract)\
                        .then_inc(jit_done, 1)
                for s in range(4):
                    dve.wait_ge(jit_hi, jit0 + s + 1)
                    nc.vector.tensor_tensor(act_lo[:, s, :], mid[:, s, :], act_hi[:, s, :].bitcast(F32),
                                            ALU.subtract).then_inc(jit_done, 1)
                with dve.Fori(0, FT // 4 - 1) as i:
                    for s in range(4):
                        jit(i, s + 4)
                        split(i * 4 + pl["c"], s + 4)
                if l < LAYERS - 1:
                    for s in range(4):
                        split(pl["c"] + FT - 4, s + 4)
                gain_ready()
                dve.wait_ge(w_used, pl["c"] + FT + W_SLOTS)
                for m in range(MT):
                    for n in range(4):
                        cols = slice(n * NB, (n + 1) * NB)
                        nc.vector.tensor_tensor(y[:, m, cols], ps[:, 4 * m + n, :], gain[:, cols], ALU.mult)\
                            .then_inc(y_scaled, 1)
                add_y(7, pl["r"] + 2)

        @block.tensor
        def _(pe):
            pe.sem_inc(w_used, W_SLOTS)
            for b in range(8):
                pe.sem_inc(bank_free[b], 1)

            def mm(dst, lhs, rhs, start=True, stop=True, loose=False):
                return nc.tensor.matmul(dst, lhs, rhs, start=start, stop=stop, skip_group_check=loose)

            def skip(b, pl, k=0):
                pe.wait_ge(bank_free[b], pl["r"] + k + 1)
                pe.sem_inc(bank_free[b], 1)
                pe.sem_inc(work_full[b], 1)

            def emptied(b, pl, k=0):
                pe.wait_ge(bank_free[b], pl["r"] + k + 1)

            def quad(c, use, q):
                for m in range(MT):
                    pe.wait_ge(bank_free[2 * q + m], use)
                for s in range(4):
                    pe.wait_ge(lo_done, c + (4 * q + s + 1 + RAW_SLOTS))
                    order = [(k, m) for k in range(4) for m in range(MT)] if s < 3 else \
                        [(k, m) for m in range(MT) for k in range(4)]
                    for k, m in order:
                        kt, tok = 4 * s + k, slice(m * P, (m + 1) * P)
                        wcols = slice(k * NB, (k + 1) * NB)
                        dst = ps[:, 2 * q + m, :]
                        mm(dst, act_hi[:, kt, tok], w_hi[:, s, wcols], kt == 0, False)
                        mm(dst, act_hi[:, kt, tok], w_lo[:, s, wcols], False, False)
                        last = mm(dst, act_lo[:, kt, tok], w_hi[:, s, wcols], False, kt == KT - 1)
                        if s == 3 and k == 3 and m == 0:
                            last.then_inc(m0_done, 1)
                    last.then_inc(w_used, 1)

            def transpose_quad(i, pl, q):
                use = i + pl["u"] + 2
                for m in range(MT):
                    pe.wait_ge(bank_free[2 * q + m], use)
                for k in range(4):
                    b = WORK + 2 * q + k // 2
                    if k % 2 == 0:
                        pe.wait_ge(bank_free[b], i + (pl["r"] + 1))
                    for m in range(MT):
                        ins = nc.tensor.transpose(ps[:, b, (k % 2) * T + m * P:(k % 2) * T + (m + 1) * P],
                                                  nat[:, q, m, k * P:(k + 1) * P], ident[:])
                    if k % 2:
                        ins.then_inc(work_full[b], 1)

            def transposed(name):
                pl = plan[name]
                with pe.Fori(0, 2) as i:
                    for q in range(2):
                        quad(i * 8 + pl["c"], i + (pl["u"] + 1), q)
                        transpose_quad(i, pl, q)

            def natural(name):
                pl = plan[name]
                with pe.Fori(0, 2) as i:
                    for q in range(2):
                        quad(i * 8 + pl["c"], i + (pl["u"] + 1), q)

            def transposes(name, ready, n0):
                pl = plan[name]
                for m in range(MT):
                    pe.wait_ge(ready, n0 + m + 1)
                    for b in range(4):
                        emptied(WORK + b, pl, m)
                        for k in range(4):
                            ins = nc.tensor.transpose(ps[:, WORK + b, k * P:(k + 1) * P],
                                                      y[:, m, (4 * b + k) * P:(4 * b + k + 1) * P], ident[:])
                        ins.then_inc(work_full[WORK + b], 1)

            def act_ready(name, rounds):
                pe.wait_ge(bank_free[7], plan[name]["r"] + rounds + 1)

            def norm(name):
                transposes(name, h_done, 2 * NORMS.index(name))
                act_ready(name, 2)

            pe.wait_ge(consts_done, 4)
            pe.wait_ge(small_in, 32)
            emptied(4, plan["vec"])
            mm(ps[:, 4, 0:16], vec_rows[0:16, :], ident[0:16, 0:16]).then_inc(work_full[4], 1)
            for b in (5, 6, 7):
                skip(b, plan["vec"])
            norm("mem_norm")
            for l in range(LAYERS):
                transposed(f"mk{l}")
                natural(f"mv{l}")
            for l in range(LAYERS):
                norm(f"pre_mix{l}")
                if l == 0:
                    transposed("sb_qk")
                    pl = plan["sb_z"]
                    for b in range(WORK, 8):
                        emptied(b, pl)
                    for h in range(SBH):
                        b = WORK + h
                        for dst, q_from, k_tile in ((slice(0, T), 0, 0), (slice(T, 384), P, 1)):
                            for d in range(2):
                                ins = mm(ps[:, b, dst], qk[:, 8 + 2 * h + d, k_tile * P:(k_tile + 1) * P],
                                         qk[:, 2 * h + d, q_from:T], d == 0, d == 1)
                        ins.then_inc(work_full[b], 1)
                    natural("sb_vu")
                    pl = plan["sb_sum"]
                    pe.wait_ge(sp_done, 1)
                    for h in range(SBH):
                        b = WORK + h
                        emptied(b, pl)
                        mm(ps[:, b, 0:P], tri[:], sp_t[:, h, 0:P])
                        mm(ps[:, b, P:T], tri[:], sp_t[:, h, P:T], True, False)
                        mm(ps[:, b, P:T], ones[:], sp_t[:, h, T:384], False, True)
                        mm(ps[:, b, T:384], tri[:], sp_t[:, h, T:384]).then_inc(work_full[b], 1)
                    pl = plan["sb_pv"]
                    pe.wait_ge(w_done, 1)
                    for b in range(4):
                        pe.wait_ge(bank_free[b], plan["sb_vu"]["u"] + 3)
                    for h in range(SBH):
                        b = WORK + h
                        emptied(b, pl)
                        for d in range(2):
                            f = slice((2 * h + d) * P, (2 * h + d + 1) * P)
                            mm(ps[:, b, d * T:(d + 1) * T], vu[:, 0, f], zs[:, h, 0:T], True, False)
                            ins = mm(ps[:, b, d * T + P:(d + 1) * T], vu[:, 1, f], zs[:, h, T:384], False, True)
                        ins.then_inc(work_full[b], 1)
                    pl = plan["pool_mean"]
                    pe.wait_ge(band_done, MT)
                    for g in range(4):
                        b = WORK + g
                        emptied(b, pl)
                        for d in range(2):
                            f = slice(SBW + (2 * g + d) * P, SBW + (2 * g + d + 1) * P)
                            for k in range(MT):
                                ins = mm(ps[:, b, d * T:(d + 1) * T], vu[:, k, f], band[:, g, k, :],
                                         k == 0, k == MT - 1)
                        ins.then_inc(work_full[b], 1)
                    pl = plan["pool_map"]
                    pe.wait_ge(pw_in, 64)
                    for b in range(WORK, 8):
                        emptied(b, pl)
                    for g in range(4):
                        b = WORK + g
                        for d in range(2):
                            for k in range(2):
                                ins = mm(ps[:, b, d * T:(d + 1) * T], pw[:, g, k, d * P:(d + 1) * P],
                                         pooled[:, 2 * g + k, :], k == 0, k == 1)
                        ins.then_inc(work_full[b], 1)
                    act_ready("pool_map", 1)
                else:
                    transposed("gla_qk")
                    pl = plan["gla_a"]
                    pe.wait_ge(gw_done, 2)
                    for m in range(MT):
                        emptied(WORK + m, pl)
                        for kt in range(KT):
                            tok = slice(m * P, (m + 1) * P)
                            dst = ps[:, WORK + m, 0:RANK]
                            mm(dst, act_hi[:, kt, tok], gw_hi[:, kt, :], kt == 0, False)
                            mm(dst, act_hi[:, kt, tok], gw_lo[:, kt, :], False, False)
                            ins = mm(dst, act_lo[:, kt, tok], gw_hi[:, kt, :], False, kt == KT - 1)
                        ins.then_inc(work_full[WORK + m], 1)
                    for b in (6, 7):
                        skip(b, pl)
                    pl = plan["gla_at"]
                    emptied(4, pl)
                    emptied(5, pl)
                    for m in range(MT):
                        ins = mm(ps[0:RANK, 4, m * P:(m + 1) * P], a_nat[:, m, :], ident[:])
                    ins.then_inc(work_full[4], 1)
                    for b in (5, 6, 7):
                        skip(b, pl)
                    pl = plan["gla_g"]
                    pe.wait_ge(gla_in, 16 * 3)
                    for b in range(WORK, 8):
                        emptied(b, pl)
                    for t in range(8):
                        b, j = WORK + t // 2, t % 2
                        ins = mm(ps[:, b, j * T:(j + 1) * T], gate_w_sb[0:RANK, t * P:(t + 1) * P], a_t[0:RANK, :])
                        if j:
                            ins.then_inc(work_full[b], 1)
                    natural("gla_v")
                    pl = plan["gla_s"]
                    pe.wait_ge(e_used, 3)
                    decayed = {(0, 2): 0, (1, 3): 1, (0, 3): 2}
                    for h in range(GH):
                        b = WORK + h
                        emptied(b, pl)
                        for ck in range(NCH):
                            for cq in range(2 * (ck // 2), NCH):
                                rows = slice(CH * (ck % 2), CH * (ck % 2 + 1))
                                col = (ck // 2) * T + cq * CH
                                for d in range(2):
                                    t = 2 * h + d
                                    if ck >= cq:
                                        lhs, rhs = ki[:, t, ck, :], qi[:, t, cq, :]
                                    else:
                                        lhs = qk[:, 8 + t, ck * CH:(ck + 1) * CH]
                                        rhs = qk[:, t, cq * CH:(cq + 1) * CH] if cq == ck + 1 else \
                                            qd[:, decayed[ck, cq], t, :]
                                    ins = mm(ps[rows, b, col:col + CH], lhs, rhs, d == 0, d == 1)
                        ins.then_inc(work_full[b], 1)
                    natural("gla_r")
                    pl = plan["gla_o"]
                    pe.wait_ge(sc_done, 2)
                    for h in range(GH):
                        for m in range(MT):
                            b = WORK + 2 * (h % 2) + m
                            emptied(b, pl, h // 2)
                            for k in range(m + 1):
                                ins = mm(ps[:, b, :], gla_sc[:, h, k, m * P:(m + 1) * P],
                                         gv[:, k, h * GV:(h + 1) * GV], k == 0, k == m)
                            ins.then_inc(work_full[b], 1)
                    transposes("gla_t", o_done, 0)
                    act_ready("gla_t", 2)
                natural(f"mix_out{l}")
                norm(f"pre_x{l}")
                transposed(f"xq{l}")
                pl = plan[f"x_s{l}"]
                pe.wait_ge(kv_in, 32 * (l + 1))
                for b in range(WORK, 8):
                    emptied(b, pl)
                for h in range(XH):
                    b = WORK + h
                    for m in range(MT):
                        for d in range(4):
                            ins = mm(ps[:, b, m * T:(m + 1) * T], qx[:, 4 * h + d, m * P:(m + 1) * P],
                                     kx[:, 4 * h + d, :], d == 0, d == 3)
                    ins.then_inc(work_full[b], 1)
                pl = plan[f"x_pt{l}"]
                for h in range(XH):
                    b = WORK + h
                    pe.wait_ge(p_done, (l * XH + h) * MT + 2)
                    emptied(b, pl)
                    for k in range(2):
                        for m in range(MT):
                            ins = nc.tensor.transpose(ps[:, b, k * T + m * P:k * T + (m + 1) * P],
                                                      px[:, h, m, k * P:(k + 1) * P], ident[:])
                    ins.then_inc(work_full[b], 1)
                pl = plan[f"x_pv{l}"]
                for b in range(WORK, 8):
                    emptied(b, pl)
                for g in range(8):
                    b = WORK + g % 4
                    emptied(b, pl, g // 4)
                    for d in range(2):
                        t = 2 * g + d
                        for k in range(2):
                            ins = mm(ps[:, b, d * T:(d + 1) * T], vx[:, k, t * P:(t + 1) * P],
                                     pxt[:, g // 2, k, :], k == 0, k == 1)
                    ins.then_inc(work_full[b], 1)
                act_ready(f"x_pv{l}", 2)
                natural(f"x_out{l}")
                norm(f"pre_ff{l}")
                pl = plan[f"gu{l}"]
                with pe.Fori(0, FF // NB) as i:
                    quad(i * 8 + pl["c"], i + (pl["u"] + 1), 0)
                    quad(i * 8 + pl["c"], i + (pl["u"] + 1), 1)
                    for m in range(MT):
                        pe.wait_ge(bank_free[2 + m], i + (pl["u"] + 2))
                    for k in range(4):
                        b = WORK + k
                        pe.wait_ge(bank_free[b], i + (pl["r"] + 1))
                        for m in range(MT):
                            ins = nc.tensor.transpose(ps[:, b, m * P:(m + 1) * P], nat[:, 0, m, k * P:(k + 1) * P],
                                                      ident[:])
                        ins.then_inc(work_full[b], 1)
                pl = plan[f"down{l}"]
                jit0 = l * FT

                def row(i, s, start):
                    pe.wait_ge(lo_done, i * 4 + (pl["c"] + s + 1 + RAW_SLOTS))
                    pe.wait_ge(jit_done, i * 4 + (jit0 + s + 1))
                    for m in range(MT):
                        tok = slice(m * P, (m + 1) * P)
                        for a, w, st in ((act_hi, w_hi, start), (act_hi, w_lo, False), (act_lo, w_hi, False)):
                            for n in range(4):
                                ins = mm(ps[:, 4 * m + n, :], a[:, s % 4, tok], w[:, s % 4, n * NB:(n + 1) * NB],
                                         st, True, True)
                    ins.then_inc(w_used, 1)
                for b in range(4):
                    pe.wait_ge(bank_free[b], pl["u"] + 1)
                for b in range(WORK, 8):
                    emptied(b, pl)
                for s in range(4):
                    row(0, s, s == 0)
                with pe.Fori(1, FT // 4) as i:
                    for s in range(4):
                        row(i, s, False)


_INS = ["x", "mem", "norms", "mem_norm", "even_w_in", "pool_w", "pool_scale", "even_w_out", "odd_w_in",
        "gla_gate_w", "gla_gate_b", "gla_gnorm", "odd_w_out", "xattn_wq", "xattn_wk", "xattn_wv", "xattn_wo",
        "ffn_w_gate", "ffn_w_up", "ffn_w_down"]
_FIRST_ONLY = {"x", "mem", "even_w_in", "pool_w", "pool_scale", "even_w_out", "odd_w_in", "gla_gate_w",
               "gla_gate_b", "gla_gnorm", "odd_w_out"}


def kernel(**inputs):
    import numpy as np
    import concourse.bacc as bacc
    from concourse.bass_utils import run_bass_kernel_spmd

    nc = bacc.Bacc("TRN2", target_bir_lowering=False, num_devices=1)
    arrays, args = {}, []
    for name in _INS:
        a = np.ascontiguousarray(inputs[name])
        arrays[f"in_{name}"] = a
        ap = nc.dram_tensor(f"in_{name}", a.shape, mybir.dt.from_np(a.dtype), kind="ExternalInput").ap()
        args.append(ap[0] if name in _FIRST_ONLY else ap)
    shape = inputs["x"].shape
    out = nc.dram_tensor("out", shape, F32, kind="ExternalOutput").ap()
    build(nc, *args, out[0])
    r = run_bass_kernel_spmd(nc, [arrays], core_ids=[0])
    return r.results[0]["out"]
```

```python
from contextlib import ExitStack

import concourse.bass as bass
from concourse import mybir

F32 = mybir.dt.float32
F32R = mybir.dt.float32r
ALU = mybir.AluOpType
ACT = mybir.ActivationFunctionType
AX_X = mybir.AxisListType.X

P = 128
NB = 512
EPS = 1e-6
MASKED = -1e4
CHUNK = 2048
W_SLOTS = 4
HALF = CHUNK // 2
RAW_SLOTS = 4
WORK = 4


def build(nc, x, mem, norms, mem_norm, even_w_in, pool_w, pool_scale, even_w_out, odd_w_in, gate_w,
          gate_b, gnorm, odd_w_out, wq, wk, wv, wo, w_gate, w_up, w_down, out):
    T, D = x.shape
    MT = T // P
    KT = D // P
    FF = w_gate.shape[2]
    FT = FF // P
    LAYERS = norms.shape[0]
    SBH, SBD = 4, 256
    SBW = SBH * SBD
    GH, GK, GV, CH = 4, 256, 512, 64
    NCH = T // CH
    RANK = gate_w.shape[0]
    XH, XD = 4, D // 4
    assert (T, D, MT, KT, LAYERS) == (256, 2048, 2, 16, 2) and FF % NB == 0

    plan = {}
    at = {"a": 0, "c": 0, "u": 0, "r": 0, "rf": 0}

    def stage(name, quads=0, rounds=0, down=False):
        plan[name] = dict(at)
        at["a"] += quads + (1 if down else 0)
        at["c"] += 4 * quads + (FT if down else 0)
        at["u"] += quads // 2 + (1 if down else 0)
        at["r"] += rounds + (1 if down else 0)
        at["rf"] += rounds

    stage("mem_norm", rounds=2)
    for l in range(LAYERS):
        stage(f"mk{l}", quads=4, rounds=2)
        stage(f"mv{l}", quads=4)
    stage("vec", rounds=1)
    for l in range(LAYERS):
        stage(f"pre_mix{l}", rounds=2)
        if l == 0:
            stage("sb_qk", quads=4, rounds=2)
            stage("sb_z", rounds=1)
            stage("sb_vu", quads=4)
            stage("sb_sum", rounds=1)
            stage("sb_pv", rounds=1)
            stage("pool_mean", rounds=1)
            stage("pool_map", rounds=1)
        else:
            stage("gla_qk", quads=4, rounds=2)
            stage("gla_a", rounds=1)
            stage("gla_at", rounds=1)
            stage("gla_g", rounds=1)
            stage("gla_v", quads=4)
            stage("gla_s", rounds=1)
            stage("gla_r", quads=4)
            stage("gla_o", rounds=GH // 2)
            stage("gla_t", rounds=2)
        stage(f"mix_out{l}", quads=4)
        stage(f"pre_x{l}", rounds=2)
        stage(f"xq{l}", quads=4, rounds=2)
        stage(f"x_s{l}", rounds=1)
        stage(f"x_pt{l}", rounds=1)
        stage(f"x_pv{l}", rounds=2)
        stage(f"x_out{l}", quads=4)
        stage(f"pre_ff{l}", rounds=2)
        stage(f"gu{l}", quads=2 * FF // NB, rounds=FF // NB)
        stage(f"down{l}", down=True)
    CHUNKS = at["c"]
    NORMS = ["mem_norm"] + [f"{n}{l}" for l in range(LAYERS) for n in ("pre_mix", "pre_x", "pre_ff")]
    POSTS = [f"{n}{l}" for l in range(LAYERS) for n in ("mix_out", "x_out", "down")]

    def cut(w, s):
        return w.rearrange("(s k p) n -> s p k n", s=4, p=P)[s]

    with ExitStack() as ctx:
        cursor = [(nc.sbuf_base + 31) // 32 * 32]

        def place(name, shape, dt, offset):
            return nc.alloc_sbuf_tensor_at(name, [P] + shape, dt, offset=offset)

        def sb(name, shape, dt=F32):
            size = 4
            for n in shape:
                size *= n
            t = place(name, shape, dt, cursor[0])
            cursor[0] += (size + 31) // 32 * 32
            return t

        def sem(name):
            return ctx.enter_context(nc.semaphore(name))

        KB = 1024
        w_raw = sb("w_raw", [RAW_SLOTS, HALF])
        w_hi = sb("w_hi", [W_SLOTS, CHUNK], F32R)
        w_lo = sb("w_lo", [W_SLOTS, CHUNK], F32R)
        xres = sb("xres", [MT, D])
        act_hi = sb("act_hi", [KT, T], F32R)
        act_lo = sb("act_lo", [KT, T], F32R)
        gain_at = cursor[0]
        gain = sb("gain", [D])
        stage_at = cursor[0]
        nat = sb("nat", [2, MT, NB])
        area = cursor[0]
        cursor[0] += 56 * KB
        pre_gain = place("pre_gain", [D], F32, stage_at)
        gate_w_sb = place("gate_w_sb", [GH * GK], F32, gain_at)
        gnorm_sb = place("gnorm_sb", [GV], F32, gain_at + 4 * KB)
        a_t = place("a_t", [T], F32, gain_at + 6 * KB)
        gw_raw = place("gw_raw", [KT, RANK], F32, gain_at + 7 * KB)
        gla_e = place("gla_e", [8, NCH, CH], F32, stage_at)
        gla_sc = place("gla_sc", [GH, MT, T], F32, stage_at)
        memx = place("memx", [MT, D], F32, area + 16 * KB)
        y = place("y", [MT, D], F32, area)
        kx = place("kx", [KT, T], F32, area + 16 * KB)
        vx = place("vx", [MT, D], F32, area + 32 * KB)
        qx = place("qx", [KT, T], F32, area)
        px = place("px", [XH, MT, T], F32, area + 48 * KB)
        pxt = px
        qk = place("qk", [KT, T], F32, area)
        vu = place("vu", [MT, D], F32, area + 16 * KB)
        zs = place("zs", [SBH, 384], F32, area + 32 * KB)
        sp_t = place("sp_t", [SBH, 384], F32, area + 38 * KB)
        band = place("band", [4, MT, T], F32, area + 44 * KB)
        pooled = place("pooled", [8, T], F32, area)
        pw = place("pw", [4, 2, 256], F32, area + 8 * KB)
        gv = place("gv", [MT, D], F32, area + 16 * KB)
        gr = place("gr", [MT, D], F32, area + 32 * KB)
        qi = place("qi", [8, NCH, CH], F32, area + 32 * KB)
        ki = place("ki", [8, NCH, CH], F32, area + 40 * KB)
        gb = place("gb", [8, NCH, CH], F32, area + 48 * KB)
        qd = place("qd", [3, 8, CH], F32, area + 48 * KB)
        gate_u = place("gate_u", [8, T], F32, area + 32 * KB)
        mid = place("mid", [FT, T], F32, area)
        ident = sb("ident", [P])
        tri = sb("tri", [P])
        ones = sb("ones", [P])
        vec_rows = sb("vec_rows", [P])
        vec = sb("vec", [16])
        gw_hi = sb("gw_hi", [KT, RANK], F32R)
        gw_lo = sb("gw_lo", [KT, RANK], F32R)
        a_nat = sb("a_nat", [MT, RANK])
        ssq_part = sb("ssq_part", [MT, 4])
        ssq = sb("ssq", [MT])
        var = sb("var", [MT])
        rstd = sb("rstd", [MT])
        half = sb("half", [8])
        xmax = sb("xmax", [XH, MT])
        xden = sb("xden", [XH, MT])
        xrec = sb("xrec", [XH, MT])
        dec = sb("dec", [8, NCH])
        dec3 = sb("dec3", [8])
        ossq = sb("ossq", [8])
        ovar = sb("ovar", [8])
        orstd = sb("orstd", [8])
        scan_m = sb("scan_m", [NCH, CH])
        assert cursor[0] <= nc.sbuf_usable_end, (cursor[0], nc.sbuf_usable_end)

        ps = ctx.enter_context(nc.psum_tensor("ps", [P, 8, NB], F32))
        kv_dram = nc.dram_tensor("kv_scratch", (LAYERS, 2, P, KT * T), F32, kind="Internal").ap()

        raw_full = [sem(f"raw_full{i}") for i in range(RAW_SLOTS)]
        raw_claimed = sem("raw_claimed")
        hi_done = sem("hi_done")
        lo_done = sem("lo_done")
        pool_lo = sem("pool_lo")
        w_used = sem("w_used")
        m0_done = sem("m0_done")
        bank_free = [sem(f"bank_free{i}") for i in range(8)]
        work_full = [None] * WORK + [sem(f"work_full{i}") for i in range(WORK, 8)]
        x_in = sem("x_in")
        mem_in = [sem(f"mem_in{m}") for m in range(MT)]
        gain_in = sem("gain_in")
        pre_gain_in = sem("pre_gain_in")
        kv_out = [sem(f"kv_out{i}") for i in range(2 * LAYERS)]
        kv_in = sem("kv_in")
        small_in = sem("small_in")
        gla_in = sem("gla_in")
        pw_in = sem("pw_in")
        y_out = sem("y_out")
        consts_done = sem("consts_done")
        vec_done = sem("vec_done")
        sq_done = sem("sq_done")
        y_scaled = sem("y_scaled")
        var_done = sem("var_done")
        rstd_done = sem("rstd_done")
        h_done = sem("h_done")
        x_done = sem("x_done")
        hi_ev = sem("hi_ev")
        jit_hi = sem("jit_hi")
        jit_done = sem("jit_done")
        z_done = sem("z_done")
        z_masked = sem("z_masked")
        l_done = sem("l_done")
        sp_done = sem("sp_done")
        w_log = sem("w_log")
        w_done = sem("w_done")
        pooled_hi = sem("pooled_hi")
        max_done = sem("max_done")
        exp_done = sem("exp_done")
        p_done = sem("p_done")
        g_done = sem("g_done")
        gate_done = sem("gate_done")
        e_done = sem("e_done")
        e_used = sem("e_used")
        sc_raw = sem("sc_raw")
        sc_done = sem("sc_done")
        osq_done = sem("osq_done")
        oroot_done = sem("oroot_done")
        gnorm_used = sem("gnorm_used")
        o_copied = sem("o_copied")
        o_done = sem("o_done")
        gw_done = sem("gw_done")
        band_done = sem("band_done")
        act_step = sem("act_step")
        dve_step = sem("dve_step")
        pool_step = sem("pool_step")

        def stepper(eng, s):
            n = [0]

            def then(ins):
                n[0] += 1
                ins.then_inc(s, 1)
                eng.wait_ge(s, n[0])
            return then

        hi_ev_at, n_ev = {}, 0
        for name, banks in ([("mem_norm", 8), ("pre_mix0", 8), ("sb_pv", 4), ("pool_map", 8), ("pre_x0", 8),
                             ("x_pv0", 8), ("pre_ff0", 8), ("pre_mix1", 8), ("gla_t", 8), ("pre_x1", 8),
                             ("x_pv1", 8), ("pre_ff1", 8)]):
            hi_ev_at[name] = n_ev
            n_ev += banks

        block = ctx.enter_context(nc.Block())

        @block.sync
        def _(sp):
            sp.sem_inc(lo_done, RAW_SLOTS)

            def load(src, c, s):
                for h in range(2):
                    slot = (2 * s + h) % RAW_SLOTS
                    sp.wait_ge(lo_done, c * 2 + (2 * s + h + 1))
                    sp.sem_inc(raw_claimed, 1)
                    if len(src.shape) == 3:
                        sp.dma_start(w_raw[:, slot, :].rearrange("p (k n) -> p k n", k=2),
                                     src[:, 2 * h:2 * h + 2, :]).then_inc(raw_full[slot], 16)
                    else:
                        sp.dma_start(w_raw[:, slot, :], src[:, h * HALF:(h + 1) * HALF])\
                            .then_inc(raw_full[slot], 16)

            def pairs(name, w, n, col0=0):
                c0 = plan[name]["c"]
                with sp.Fori(0, n) as i:
                    for q in range(2):
                        for s in range(4):
                            src = cut(w, s)[:, :, bass.ds(i * (2 * NB) + (col0 + q * NB), NB)]
                            load(src, i * 8 + c0, 4 * q + s)

            for l in range(LAYERS):
                pairs(f"mk{l}", wk[l], 2)
                pairs(f"mv{l}", wv[l], 2)
            for l in range(LAYERS):
                if l == 0:
                    pairs("sb_qk", even_w_in, 2)
                    pairs("sb_vu", even_w_in, 2, 2 * SBW)
                    pairs("mix_out0", even_w_out, 2)
                else:
                    pairs("gla_qk", odd_w_in, 2)
                    pairs("gla_v", odd_w_in, 2, 2 * GH * GK)
                    pairs("gla_r", odd_w_in, 2, 2 * GH * GK + GH * GV)
                    pairs("mix_out1", odd_w_out, 2)
                pairs(f"xq{l}", wq[l], 2)
                pairs(f"x_out{l}", wo[l], 2)
                c0 = plan[f"gu{l}"]["c"]
                with sp.Fori(0, FF // NB) as i:
                    for q, w in enumerate((w_gate[l], w_up[l])):
                        for s in range(4):
                            load(cut(w, s)[:, :, bass.ds(i * NB, NB)], i * 8 + c0, 4 * q + s)
                c0 = plan[f"down{l}"]["c"]
                wd = w_down[l].rearrange("(i s p) n -> s p i n", s=4, p=P)
                with sp.Fori(0, FT // 4) as i:
                    for s in range(4):
                        load(wd[s][:, bass.ds(i, 1), :].rearrange("p o n -> p (o n)"), i * 4 + c0, s)
            for m in range(MT):
                sp.wait_ge(x_done, 2 * len(POSTS) - 1 + m)
                sp.dma_start(out[m * P:(m + 1) * P, :], xres[:, m, :]).then_inc(y_out, 16)
            sp.wait_ge(y_out, 16 * MT)

        @block.gpsimd
        def _(pool):
            then = stepper(pool, pool_step)

            def load_gain(row):
                pool.dma_start(gain[:], row.partition_broadcast(P)).then_inc(gain_in, 16)

            def load_pre_gain(row):
                pool.dma_start(pre_gain[:], row.partition_broadcast(P)).then_inc(pre_gain_in, 16)

            load_pre_gain(mem_norm)
            load_gain(norms[0, 0])
            then(nc.gpsimd.memset(ident[:], 0.0))
            nc.gpsimd.affine_select(out=ident[:], in_=ident[:], compare_op=ALU.not_equal, fill=1.0, base=0,
                                    pattern=[[-1, P]], channel_multiplier=1).then_inc(consts_done, 1)
            nc.gpsimd.memset(half[:], -0.5).then_inc(consts_done, 1)
            nc.gpsimd.memset(ones[:], 1.0).then_inc(consts_done, 1)
            pool.wait_ge(consts_done, 3)
            nc.gpsimd.affine_select(out=tri[:], in_=ones[:], compare_op=ALU.is_ge, fill=0.0, base=0,
                                    pattern=[[-1, P]], channel_multiplier=1).then_inc(consts_done, 1)
            then(nc.gpsimd.memset(scan_m[:], 1.0))
            then(nc.gpsimd.memset(scan_m[:, :, 0:1], 0.0))

            n_roots = [0]

            def roots(ms):
                for m in ms:
                    n_roots[0] += 1
                    pool.wait_ge(var_done, n_roots[0])
                    nc.gpsimd.tensor_tensor(rstd[:, m:m + 1], var[:, m:m + 1], half[:, 0:1], ALU.pow)\
                        .then_inc(rstd_done, 1)

            def turn_roots(c):
                for m in range(MT):
                    roots([m])
                    if m == 1:
                        lo_split(c, 2, (0,))
                    roots([m])
                    if m == 0:
                        lo_split(c, 1, (0, 1))

            def lo_split(c, s, halves):
                for h in halves:
                    part = slice(h * HALF, (h + 1) * HALF)
                    pool.wait_ge(hi_done, 2 * (c + s) + h + 1)
                    nc.gpsimd.tensor_tensor(w_lo[:, s, part], w_raw[:, (2 * s + h) % RAW_SLOTS, :],
                                            w_hi[:, s, part].bitcast(F32), ALU.subtract).then_inc(pool_lo, 1)

            roots([0, 1])
            roots([0, 1])
            pool.wait_ge(h_done, 4)
            load_gain(norms[0, 1])
            pool.wait_ge(work_full[7], plan[f"mk{LAYERS - 1}"]["rf"] + 2)
            for s_kv in kv_out:
                pool.wait_ge(s_kv, 16)
            for g in range(4):
                nc.gpsimd.memset(band[:, g, :, :], 1.0 / (2 << g)).then_inc(pool_step, 1)
            pool.wait_ge(pool_step, 3 + 4)
            for t in range((2 << 3) - 1):
                g0 = [g for g in range(4) if (2 << g) > t + 1][0]
                nc.gpsimd.memset(band[:, g0:4, :, t:t + 1], 1.0 / (t + 1)).then_inc(pool_step, 1)
            base = 3 + 4 + (2 << 3) - 1
            pool.wait_ge(pool_step, base)
            nc.gpsimd.affine_select(out=band[:], in_=band[:], compare_op=ALU.is_ge, fill=0.0, base=0,
                                    pattern=[[0, 4], [-P, MT], [1, T]], channel_multiplier=-1)\
                .then_inc(pool_step, 1)
            pool.wait_ge(pool_step, base + 1)
            for g in range(4):
                nc.gpsimd.affine_select(out=band[:, g, :, :], in_=band[:, g, :, :], compare_op=ALU.is_ge,
                                        fill=0.0, base=(2 << g) - 1, pattern=[[P, MT], [-1, T]],
                                        channel_multiplier=1).then_inc(consts_done, 1)
            for part, n_q in ((slice(0, T), T), (slice(T, 384), P)):
                pool.wait_ge(z_done, SBH)
                nc.gpsimd.affine_select(out=zs[:, :, part], in_=zs[:, :, part], compare_op=ALU.is_gt,
                                        fill=MASKED, base=0, pattern=[[0, SBH], [1, n_q]],
                                        channel_multiplier=-1).then_inc(z_masked, 1)
            pool.wait_ge(z_done, SBH)
            for g in range(4):
                pool.dma_start(pw[:, g, :, :], pool_w[g].rearrange("(k p) n -> p k n", p=P))\
                    .then_inc(pw_in, 16)
            y_banks = 0
            for l in range(LAYERS):
                if l == 0:
                    load_pre_gain(norms[0, 2])
                else:
                    pool.wait_ge(sc_raw, 2 * GH)
                    for t, q0 in ((0, 0), (1, P)):
                        part = gla_sc[:, :, t, q0:T]
                        nc.gpsimd.affine_select(out=part, in_=part, compare_op=ALU.is_ge, fill=0.0, base=0,
                                                pattern=[[0, GH], [1, T - q0]], channel_multiplier=-1)\
                            .then_inc(sc_done, 1)
                    pool.wait_ge(osq_done, 1)
                    nc.gpsimd.tensor_tensor(orstd[:], ovar[:], half[:], ALU.pow).then_inc(oroot_done, 1)
                    pool.wait_ge(gnorm_used, 1)
                    load_gain(norms[1, 1])
                    load_pre_gain(norms[1, 2])
                if l == 0:
                    pool.wait_ge(bank_free[7], plan["pool_map"]["r"] + 2)
                else:
                    pool.wait_ge(o_done, 2 * MT)
                for s_kv in kv_out:
                    pool.wait_ge(s_kv, 16)
                pool.dma_start(kx[:].rearrange("p k t -> p (k t)"), kv_dram[l, 0]).then_inc(kv_in, 16)
                pool.dma_start(vx[:].rearrange("p m n -> p (m n)"), kv_dram[l, 1]).then_inc(kv_in, 16)
                turn_roots(plan[f"xq{l}"]["c"])
                y_banks += 8
                pool.wait_ge(y_scaled, y_banks)
                load_gain(norms[l, 3])
                pool.wait_ge(max_done, (l + 1) * XH * MT)
                load_pre_gain(norms[l, 4])
                turn_roots(plan[f"gu{l}"]["c"])
                y_banks += 8
                pool.wait_ge(y_scaled, y_banks)
                load_gain(norms[l, 5])
                if l < LAYERS - 1:
                    pool.wait_ge(work_full[7], plan[f"gu{l}"]["rf"] + FF // NB)
                    load_pre_gain(norms[l + 1, 0])
                    turn_roots(plan["gla_qk"]["c"])
                    y_banks += 8
                    pool.wait_ge(y_scaled, y_banks)
                    pool.dma_start(gate_w_sb[0:RANK, :], gate_w).then_inc(gla_in, 16)
                    pool.dma_start(gnorm_sb[:], gnorm.partition_broadcast(P)).then_inc(gla_in, 16)
                    pool.dma_start(gw_raw[:], odd_w_in[:, 2 * GH * (GK + GV):].rearrange(
                        "(k p) n -> p k n", p=P)).then_inc(gla_in, 16)
                else:
                    roots([0, 1])

        @block.scalar
        def _(act):
            then = stepper(act, act_step)
            for m in range(MT):
                act.dma_start(memx[:, m, :], mem[m * P:(m + 1) * P, :]).then_inc(mem_in[m], 16)
            act.dma_start(vec_rows[0:8, :], pool_scale.rearrange("(k p) -> k p", p=P)).then_inc(small_in, 16)
            act.dma_start(vec_rows[8:16, :], gate_b.rearrange("(k p) -> k p", p=P)).then_inc(small_in, 16)
            act.dma_start(xres[:], x.rearrange("(m p) n -> p m n", p=P)).then_inc(x_in, 16)

            def split(c, s):
                act.wait_ge(w_used, c + (s + 1))
                for h in range(2):
                    slot = (2 * s + h) % RAW_SLOTS
                    act.wait_ge(raw_full[slot], c * 8 + (16 * ((2 * s + h) // RAW_SLOTS) + 16))
                    nc.scalar.activation(w_hi[:, s % W_SLOTS, h * HALF:(h + 1) * HALF], w_raw[:, slot, :],
                                         ACT.Copy).then_inc(hi_done, 1)

            def square_x(name, m, src=xres):
                nc.scalar.activation(y[:, m, :], src[:, m, :], ACT.Square, accum_out=ssq[:, m:m + 1])\
                    .then_inc(sq_done, 1)

            def round_transposes(name, m):
                pl = plan[name]
                for b in range(4):
                    act.wait_ge(work_full[WORK + b], pl["rf"] + m + 1)
                    nc.scalar.activation(
                        act_hi[:, 4 * b:4 * b + 4, m * P:(m + 1) * P],
                        ps[:, WORK + b, :].rearrange("p (k t) -> p k t", t=P), ACT.Copy).then_inc(hi_ev, 1)

            def pair(c, evac0, mid_pair, evac1, end_pair, after_first=None):
                split(c, 4)
                if after_first is not None:
                    after_first()
                split(c, 5)
                split(c, 6)
                evac0()
                split(c, 7)
                split(c, 8)
                mid_pair()
                split(c, 9)
                split(c, 10)
                evac1()
                end_pair()
                split(c, 11)

            nothing = lambda: None

            def take_m0(i, pl, q, dst, func=ACT.Copy, reuse=None):
                def run():
                    act.wait_ge(m0_done, i * 2 + (pl["a"] + q + 1))
                    if reuse is not None:
                        act.wait_ge(*reuse)
                    nc.scalar.activation(dst, ps[:, 2 * q, :], func).then_inc(bank_free[2 * q], 1)
                return run

            def transposed(name, dst, tile0=0):
                pl = plan[name]
                with act.Fori(0, 2) as i:
                    def take_t(q):
                        def run():
                            b = WORK + 2 * q
                            act.wait_ge(work_full[b], i + (pl["rf"] + 1))
                            nc.scalar.activation(dst[:, bass.ds(i * 8 + (tile0 + 4 * q), 2), :],
                                                 ps[:, b, :].rearrange("p (k t) -> p k t", t=T), ACT.Copy)\
                                .then_inc(bank_free[b], 1)
                        return run

                    def reuse(q):
                        return (work_full[WORK + 2 * q + 1], i + pl["rf"]) if pl["rf"] else None
                    pair(i * 8 + pl["c"],
                         take_m0(i, pl, 0, nat[:, 0, 0, :], reuse=reuse(0)), take_t(0),
                         take_m0(i, pl, 1, nat[:, 1, 0, :], reuse=reuse(1)), take_t(1))

            def natural(name, dst, pairs=None, mid=nothing, end=nothing):
                pl = plan[name]

                def one(i):
                    pair(i * 8 + pl["c"],
                         take_m0(i, pl, 0, dst[:, 0, bass.ds(i * (2 * NB), NB)]), mid,
                         take_m0(i, pl, 1, dst[:, 0, bass.ds(i * (2 * NB) + NB, NB)]), end)
                if pairs is None:
                    with act.Fori(0, 2) as i:
                        one(i)
                else:
                    for i in pairs:
                        one(i)

            banks_squared = [0]

            def square_banks(banks, m):
                for b, part in banks:
                    banks_squared[0] += 1
                    act.wait_ge(y_scaled, banks_squared[0])
                    bank = ps[:, b, :]
                    nc.scalar.activation(bank, bank, ACT.Square, accum_out=ssq_part[:, m, part:part + 1])\
                        .then_inc(bank_free[b], 1)

            xs_squared = [0]

            def turn(c, last, nxt):
                square_banks(last[0], 0)
                if c is not None:
                    split(c, 0)
                if nxt is not None:
                    act.wait_ge(x_done, xs_squared[0] + 1)
                    square_x(nxt, 0)
                    split(c, 1)
                in_work = last[1][0][0] >= WORK
                if nxt is not None and not in_work:
                    round_transposes(nxt, 0)
                square_banks(last[1], 1)
                if nxt is not None:
                    if in_work:
                        round_transposes(nxt, 0)
                    split(c, 2)
                    split(c, 3)
                    act.wait_ge(x_done, xs_squared[0] + 2)
                    square_x(nxt, 1)
                    round_transposes(nxt, 1)
                xs_squared[0] += 2

            def output(name, nxt):
                c = plan[name]["c"]
                pair(c, lambda: (square_banks([(0, 0)], 0), square_banks([(1, 0)], 1)), nothing,
                     lambda: (square_banks([(2, 1)], 0), square_banks([(3, 1)], 1)), nothing)
                for s in (12, 13, 14):
                    split(c, s)
                square_banks([(0, 2)], 0)
                square_banks([(1, 2)], 1)
                split(c, 15)
                turn(c + 16, ([(2, 3)], [(3, 3)]), nxt)

            def round_tiles(name, banks, first_tile, n_tiles, scale=None):
                pl = plan[name]
                for k, (b, rnd) in enumerate(banks):
                    act.wait_ge(work_full[b], pl["rf"] + rnd + 1)
                    if scale is None:
                        nc.scalar.activation(act_hi[:, first_tile + 2 * k:first_tile + 2 * k + 2, :],
                                             ps[:, b, :].rearrange("p (k t) -> p k t", t=T), ACT.Copy)\
                            .then_inc(hi_ev, 1)
                    else:
                        for j in range(2):
                            t = 2 * k + j
                            nc.scalar.activation(act_hi[:, first_tile + t, :], ps[:, b, j * T:(j + 1) * T],
                                                 ACT.Copy, scale=scale[:, t:t + 1]).then_inc(hi_ev, 1)

            act.wait_ge(mem_in[0], 16)
            square_x("mem_norm", 0, memx)
            split(0, 0)
            act.wait_ge(mem_in[1], 16)
            square_x("mem_norm", 1, memx)
            round_transposes("mem_norm", 0)
            split(0, 1)
            split(0, 2)
            split(0, 3)
            round_transposes("mem_norm", 1)
            act.wait_ge(x_in, 16)
            for m in range(MT):
                square_x("pre_mix0", m)
            for l in range(LAYERS):
                if l:
                    act.wait_ge(kv_out[2 * l - 2], 16)
                transposed(f"mk{l}", kx)
                pl = plan[f"mk{l}"]
                for b in range(WORK, 8):
                    act.wait_ge(bank_free[b], pl["r"] + 3)
                act.dma_start(kv_dram[l, 0], kx[:].rearrange("p k t -> p (k t)")).then_inc(kv_out[2 * l], 16)
                if l:
                    act.wait_ge(kv_out[2 * l - 1], 16)
                natural(f"mv{l}", vx)
                pl = plan[f"mv{l}"]
                for b in range(4):
                    act.wait_ge(bank_free[b], pl["u"] + 3)
                act.dma_start(kv_dram[l, 1], vx[:].rearrange("p m n -> p (m n)")).then_inc(kv_out[2 * l + 1], 16)

            for l in range(LAYERS):
                if l == 0:
                    for m in range(MT):
                        round_transposes("pre_mix0", m)
                    transposed("sb_qk", qk)
                    pl = plan["sb_z"]
                    for s_kv in kv_out:
                        act.wait_ge(s_kv, 16)
                    for h in range(SBH):
                        act.wait_ge(work_full[WORK + h], pl["rf"] + 1)
                        nc.scalar.activation(zs[:, h, :], ps[:, WORK + h, 0:384], ACT.Copy, scale=SBD ** -0.5)\
                            .then_inc(z_done, 1)
                        act.wait_ge(z_done, h + 1)
                        act.sem_inc(bank_free[WORK + h], 1)
                    act.wait_ge(z_masked, 2)
                    then(nc.scalar.activation(sp_t[:], zs[:], ACT.Abs))
                    then(nc.scalar.activation(sp_t[:], sp_t[:], ACT.Exp, scale=-1.0))
                    nc.scalar.activation(sp_t[:], sp_t[:], ACT.Ln, bias=1.0).then_inc(l_done, 1)
                    natural("sb_vu", vu, pairs=[0])
                    act.wait_ge(w_log, SBH)
                    nc.scalar.activation(zs[:], zs[:], ACT.Exp).then_inc(w_done, 1)
                    natural("sb_vu", vu, pairs=[1])
                    round_tiles("sb_pv", [(WORK + h, 0) for h in range(SBH)], 0, 8)
                    pl = plan["pool_mean"]
                    for b in (4, 6):
                        act.wait_ge(work_full[b], pl["rf"] + 1)
                        nc.scalar.activation(pooled[:, 2 * (b - WORK):2 * (b - WORK) + 2, :],
                                             ps[:, b, :].rearrange("p (k t) -> p k t", t=T), ACT.Copy)\
                            .then_inc(bank_free[b], 1)
                    act.wait_ge(vec_done, 1)
                    round_tiles("pool_map", [(WORK + g, 0) for g in range(4)], 8, 8, scale=vec[:, 0:8])
                else:
                    transposed("gla_qk", qk)
                    act.wait_ge(gla_in, 16 * 3)
                    nc.scalar.activation(gw_hi[:], gw_raw[:], ACT.Copy).then_inc(gw_done, 1)
                    pl = plan["gla_g"]
                    for t in range(8):
                        b, j = WORK + t // 2, t % 2
                        act.wait_ge(work_full[b], pl["rf"] + 1)
                        nc.scalar.activation(gb[:, t, :, :].rearrange("p c t -> p (c t)"),
                                             ps[:, b, j * T:(j + 1) * T], ACT.Abs, bias=vec[:, 8 + t:9 + t])\
                            .then_inc(g_done, 1)
                    act.wait_ge(g_done, 8)
                    then(nc.scalar.activation(gb[:], gb[:], ACT.Exp, scale=-1.0))
                    nc.scalar.activation(gb[:], gb[:], ACT.Ln, bias=1.0).then_inc(g_done, 1)
                    s16 = 1.0 / 16.0
                    act.wait_ge(gate_done, 1)
                    then(nc.scalar.activation(qi[:], gla_e[:], ACT.Exp, scale=s16))
                    nc.scalar.activation(ki[:], gla_e[:], ACT.Exp, scale=-s16).then_inc(e_done, 1)

                    def exp_state():
                        act.wait_ge(e_used, 1)
                        nc.scalar.activation(gla_e[:], gla_e[:], ACT.Exp, scale=s16).then_inc(e_done, 1)
                        nc.scalar.activation(dec[:], gb[:, :, :, CH - 1], ACT.Exp, scale=s16).then_inc(e_done, 1)

                    def exp_query():
                        act.wait_ge(e_used, 2)
                        nc.scalar.activation(gla_e[:], gb[:], ACT.Exp, scale=s16).then_inc(e_done, 1)
                    natural("gla_v", gv, pairs=[0], mid=exp_state)
                    natural("gla_v", gv, pairs=[1], mid=exp_query)
                    pl = plan["gla_s"]
                    act.wait_ge(e_used, 3)
                    for h in range(GH):
                        act.wait_ge(work_full[WORK + h], pl["rf"] + 1)
                        nc.scalar.activation(gla_sc[:, h, 0, :], ps[:, WORK + h, 0:T], ACT.Copy)\
                            .then_inc(sc_raw, 1)
                        nc.scalar.activation(gla_sc[:, h, 1, P:T], ps[:, WORK + h, T + P:2 * T], ACT.Copy)\
                            .then_inc(sc_raw, 1)
                        act.wait_ge(sc_raw, 2 * h + 2)
                        act.sem_inc(bank_free[WORK + h], 1)
                    def silu_r(i, q):
                        pr = plan["gla_r"]

                        def run():
                            for m in range(MT):
                                if m == 0:
                                    act.wait_ge(m0_done, i * 2 + (pr["a"] + q + 1))
                                else:
                                    act.wait_ge(w_used, i * 8 + (pr["c"] + 4 * q + 4 + W_SLOTS))
                                nc.scalar.activation(gr[:, m, bass.ds(i * (2 * NB) + q * NB, NB)],
                                                     ps[:, 2 * q + m, :], ACT.Silu)\
                                    .then_inc(bank_free[2 * q + m], 1)
                        return run
                    pair(plan["gla_r"]["c"], silu_r(0, 0), nothing, silu_r(0, 1), nothing)
                    pl = plan["gla_o"]
                    for h in range(GH):
                        for m in range(MT):
                            b = WORK + 2 * (h % 2) + m
                            act.wait_ge(o_copied, 2 * h + m + 1)
                            nc.scalar.activation(ps[:, b, :], ps[:, b, :], ACT.Square,
                                                 accum_out=ossq[:, 2 * h + m:2 * h + m + 1])\
                                .then_inc(bank_free[b], 1)
                    pair(plan["gla_r"]["c"] + 8, silu_r(1, 0), nothing, silu_r(1, 1), nothing)
                    for m in range(MT):
                        round_transposes("gla_t", m)
                output(f"mix_out{l}", f"pre_x{l}")
                transposed(f"xq{l}", qx)
                for h in range(XH):
                    for m in range(MT):
                        k = (l * XH + h) * MT + m
                        act.wait_ge(max_done, k + 1)
                        nc.scalar.activation(px[:, h, m, :], ps[:, WORK + h, m * T:(m + 1) * T], ACT.Exp,
                                             bias=xmax[:, h, m:m + 1], scale=XD ** -0.5,
                                             accum_out=xden[:, h, m:m + 1]).then_inc(exp_done, 1)
                    act.wait_ge(exp_done, (l * XH + h) * MT + 2)
                    act.sem_inc(bank_free[WORK + h], 1)
                pl = plan[f"x_pt{l}"]
                for b in (4, 6):
                    act.wait_ge(work_full[7], pl["rf"] + 1)
                    act.wait_ge(work_full[b], pl["rf"] + 1)
                    nc.scalar.activation(pxt[:, b - WORK, :, :],
                                         ps[:, b, :].rearrange("p (k t) -> p k t", t=T), ACT.Copy)\
                        .then_inc(bank_free[b], 1)
                round_tiles(f"x_pv{l}", [(WORK + k % 4, k // 4) for k in range(8)], 0, 16)
                output(f"x_out{l}", f"pre_ff{l}")
                pl = plan[f"gu{l}"]
                def silu(i):
                    def run():
                        for m in range(MT):
                            if m == 0:
                                act.wait_ge(m0_done, i * 2 + (pl["a"] + 1))
                            else:
                                act.wait_ge(w_used, i * 8 + (pl["c"] + 4 + W_SLOTS))
                            act.wait_ge(bank_free[2 + m], i + (pl["u"] + 1))
                            nc.scalar.activation(nat[:, 1, m, :], ps[:, m, :], ACT.Silu)\
                                .then_inc(bank_free[m], 1)
                    return run

                def take_mid(i, k=0):
                    def run():
                        for b in (4, 6):
                            act.wait_ge(work_full[b], i + (pl["rf"] + 1 - k))
                            nc.scalar.activation(mid[:, bass.ds(i * 4 + (b - WORK - 4 * k), 1), :],
                                                 ps[:, b:b + 1, 0:T], ACT.Copy).then_inc(bank_free[b], 1)
                    return run
                pair(pl["c"], silu(0), nothing, nothing, nothing)
                with act.Fori(1, FF // NB) as i:
                    pair(i * 8 + pl["c"], silu(i), nothing, nothing, nothing, take_mid(i, 1))
                take_mid(FF // NB - 1)()
                pu, pl = pl, plan[f"down{l}"]
                jit0 = l * FT
                for b in range(WORK, 8):
                    act.wait_ge(bank_free[b], pl["r"] + 1)

                def jit(i, s):
                    act.wait_ge(w_used, i * 4 + (pl["c"] + s - 4 + 1 + W_SLOTS))
                    nc.scalar.activation(act_hi[:, s % 4:s % 4 + 1, :], mid[:, bass.ds(i * 4 + s, 1), :],
                                         ACT.Copy).then_inc(jit_hi, 1)
                act.wait_ge(w_used, pl["c"] + W_SLOTS)
                for s in range(4):
                    nc.scalar.activation(act_hi[:, s, :], mid[:, s, :], ACT.Copy).then_inc(jit_hi, 1)
                with act.Fori(0, FT // 4 - 1) as i:
                    for s in range(4):
                        jit(i, s + 4)
                        split(i * 4 + pl["c"], s + 4)
                more = l < LAYERS - 1
                turn(pl["c"] + FT if more else None, [[(4 * m + n, n) for n in range(4)] for m in range(MT)],
                     f"pre_mix{l + 1}" if more else None)

        @block.vector
        def _(dve):
            then = stepper(dve, dve_step)

            def split(c, s, halves=(0, 1)):
                for h in halves:
                    part = slice(h * HALF, (h + 1) * HALF)
                    dve.wait_ge(hi_done, c * 2 + (2 * s + h + 1))
                    nc.vector.tensor_tensor(w_lo[:, s % W_SLOTS, part], w_raw[:, (2 * s + h) % RAW_SLOTS, :],
                                            w_hi[:, s % W_SLOTS, part].bitcast(F32), ALU.subtract)\
                        .then_inc(lo_done, 1)

            pool_halves = [0]

            def pool_split(n):
                pool_halves[0] += n
                dve.wait_ge(pool_lo, pool_halves[0])
                dve.sem_inc(lo_done, n)

            n_roots = [0]

            def root(m):
                nc.vector.tensor_scalar(var[:, m:m + 1], ssq[:, m:m + 1], 1.0 / D, EPS, ALU.mult, ALU.add)\
                    .then_inc(var_done, 1)
                n_roots[0] += 1

            def root_ready():
                dve.wait_ge(rstd_done, n_roots[0])

            gains = [0, 0]

            def gain_ready(kind=0):
                gains[kind] += 1
                dve.wait_ge((gain_in, pre_gain_in)[kind], 16 * gains[kind])

            def normed(m, src, g):
                nc.vector.scalar_tensor_tensor(out=y[:, m, :], in0=src[:, m, :], scalar=rstd[:, m:m + 1],
                                               in1=g[:], op0=ALU.mult, op1=ALU.mult).then_inc(h_done, 1)

            n_sq = [0]

            def x_root(m):
                n_sq[0] += 1
                dve.wait_ge(sq_done, n_sq[0])
                root(m)

            def rest_transposes(name, m, banks=range(4)):
                e0 = hi_ev_at[name]
                for b in banks:
                    dve.wait_ge(hi_ev, e0 + 4 * m + b + 1)
                    sl = (slice(None), slice(4 * b, 4 * b + 4), slice(m * P, (m + 1) * P))
                    nc.vector.tensor_tensor(act_lo[sl], ps[:, WORK + b, :].rearrange("p (k t) -> p k t", t=P),
                                            act_hi[sl].bitcast(F32), ALU.subtract)\
                        .then_inc(bank_free[WORK + b], 1)

            def pair(c, evac0, mid_pair, evac1, end_pair, after_first=None):
                split(c, 4)
                if after_first is not None:
                    after_first()
                split(c, 5)
                split(c, 6)
                evac0()
                split(c, 7)
                split(c, 8)
                mid_pair()
                split(c, 9)
                split(c, 10)
                evac1()
                end_pair()
                split(c, 11)

            nothing = lambda: None

            def take_m1(i, pl, q, dst, reuse=None):
                def run():
                    dve.wait_ge(w_used, i * 8 + (pl["c"] + 4 * q + 4 + W_SLOTS))
                    if reuse is not None:
                        dve.wait_ge(*reuse)
                    nc.vector.tensor_copy(dst, ps[:, 2 * q + 1, :]).then_inc(bank_free[2 * q + 1], 1)
                return run

            def transposed(name, dst):
                pl = plan[name]
                with dve.Fori(0, 2) as i:
                    def take_t(q):
                        def run():
                            b = WORK + 2 * q + 1
                            dve.wait_ge(work_full[b], i + (pl["rf"] + 1))
                            nc.vector.tensor_copy(dst[:, bass.ds(i * 8 + (4 * q + 2), 2), :],
                                                  ps[:, b, :].rearrange("p (k t) -> p k t", t=T))\
                                .then_inc(bank_free[b], 1)
                        return run

                    def reuse(q):
                        return (work_full[WORK + 2 * q + 1], i + pl["rf"]) if pl["rf"] else None
                    pair(i * 8 + pl["c"],
                         take_m1(i, pl, 0, nat[:, 0, 1, :], reuse(0)), take_t(0),
                         take_m1(i, pl, 1, nat[:, 1, 1, :], reuse(1)), take_t(1))

            def natural(name, dst, pairs=None, mid=nothing, end=nothing):
                pl = plan[name]

                def one(i):
                    pair(i * 8 + pl["c"],
                         take_m1(i, pl, 0, dst[:, 1, bass.ds(i * (2 * NB), NB)]), mid,
                         take_m1(i, pl, 1, dst[:, 1, bass.ds(i * (2 * NB) + NB, NB)]), end)
                if pairs is None:
                    with dve.Fori(0, 2) as i:
                        one(i)
                else:
                    for i in pairs:
                        one(i)

            def scale_bank(b, m, col):
                cols = slice(col, col + NB)
                nc.vector.tensor_tensor(y[:, m, cols], ps[:, b, :], gain[:, cols], ALU.mult).then_inc(y_scaled, 1)

            def x_update(m):
                nc.vector.scalar_tensor_tensor(out=xres[:, m, :], in0=y[:, m, :], scalar=rstd[:, m:m + 1],
                                               in1=xres[:, m, :], op0=ALU.mult, op1=ALU.add).then_inc(x_done, 1)

            def turn(c, last, ready, freed, nxt):
                def output_root(m, between=lambda: None):
                    dve.wait_ge(*ready[m])
                    for b, col in last[m]:
                        scale_bank(b, m, col)
                    between()
                    for f in freed[m]:
                        dve.wait_ge(*f)
                    then(nc.vector.tensor_reduce(ssq[:, m:m + 1], ssq_part[:, m, :], AX_X, ALU.add))
                    root(m)
                output_root(0)
                root_ready()
                x_update(0)
                if nxt is not None:
                    split(c, 0)
                    x_root(0)
                    root_ready()
                    gain_ready(1)
                    normed(0, xres, pre_gain)
                    pool_split(2)
                early = 2 if nxt is not None and last[1][0][0] < WORK else 0
                output_root(1, (lambda: rest_transposes(nxt, 0, range(early))) if early else (lambda: None))
                if nxt is not None:
                    rest_transposes(nxt, 0, range(early, 4))
                root_ready()
                x_update(1)
                if nxt is not None:
                    pool_split(1)
                    split(c, 2, (1,))
                    split(c, 3, (0,))
                    x_root(1)
                    split(c, 3, (1,))
                    root_ready()
                    normed(1, xres, pre_gain)
                    rest_transposes(nxt, 1)

            def output(name, nxt):
                pl = plan[name]
                c = pl["c"]
                gain_ready()

                def scale(i, q):
                    def run():
                        for m in range(MT):
                            if m == 0:
                                dve.wait_ge(m0_done, pl["a"] + 2 * i + q + 1)
                            else:
                                dve.wait_ge(w_used, c + 8 * i + 4 * q + 4 + W_SLOTS)
                            scale_bank(2 * q + m, m, (2 * i + q) * NB)
                    return run
                pair(c, scale(0, 0), nothing, scale(0, 1), nothing)
                for s in (12, 13, 14):
                    split(c, s)
                scale(1, 0)()
                split(c, 15)
                turn(c + 16, [[(2, 3 * NB)], [(3, 3 * NB)]],
                     [(m0_done, pl["a"] + 4), (w_used, c + 16 + W_SLOTS)],
                     [[(bank_free[m], pl["u"] + 3), (bank_free[2 + m], pl["u"] + 3)] for m in range(MT)], nxt)

            def rest_tiles(name, banks, first_tile, scale=None):
                e0 = hi_ev_at[name]
                for k, b in enumerate(banks):
                    if scale is None:
                        dve.wait_ge(hi_ev, e0 + k + 1)
                        sl = slice(first_tile + 2 * k, first_tile + 2 * k + 2)
                        nc.vector.tensor_tensor(act_lo[:, sl, :], ps[:, b, :].rearrange("p (k t) -> p k t", t=T),
                                                act_hi[:, sl, :].bitcast(F32), ALU.subtract)\
                            .then_inc(bank_free[b], 1)
                    else:
                        for j in range(2):
                            t = 2 * k + j
                            dve.wait_ge(hi_ev, e0 + 2 * k + 2)
                            ins = nc.vector.scalar_tensor_tensor(
                                out=act_lo[:, first_tile + t, :], in0=ps[:, b, j * T:(j + 1) * T],
                                scalar=scale[:, t:t + 1], in1=act_hi[:, first_tile + t, :].bitcast(F32),
                                op0=ALU.mult, op1=ALU.subtract)
                        ins.then_inc(bank_free[b], 1)

            gain_ready(1)
            x_root(0)
            root_ready()
            normed(0, memx, pre_gain)
            split(0, 0)
            rest_transposes("mem_norm", 0)
            x_root(1)
            split(0, 1)
            root_ready()
            normed(1, memx, pre_gain)
            split(0, 2)
            split(0, 3)
            rest_transposes("mem_norm", 1)
            gain_ready()
            for m in range(MT):
                x_root(m)
                root_ready()
                normed(m, xres, gain)
            for l in range(LAYERS):
                if l:
                    dve.wait_ge(kv_out[2 * l - 2], 16)
                transposed(f"mk{l}", kx)
                if l:
                    dve.wait_ge(kv_out[2 * l - 1], 16)
                natural(f"mv{l}", vx)

            dve.wait_ge(work_full[4], plan["vec"]["rf"] + 1)
            nc.vector.tensor_copy(vec[:], ps[:, 4, 0:16]).then_inc(vec_done, 1)
            dve.wait_ge(vec_done, 1)
            dve.sem_inc(bank_free[4], 1)
            for l in range(LAYERS):
                if l == 0:
                    for m in range(MT):
                        rest_transposes("pre_mix0", m)
                    transposed("sb_qk", qk)
                    dve.wait_ge(l_done, 1)
                    nc.vector.scalar_tensor_tensor(out=sp_t[:], in0=zs[:], scalar=0.0, in1=sp_t[:],
                                                   op0=ALU.max, op1=ALU.add).then_inc(sp_done, 1)
                    dve.wait_ge(consts_done, 8)
                    for k in range(MT):
                        nc.vector.tensor_tensor(band[:, :, k, k * P:(k + 1) * P], band[:, :, k, k * P:(k + 1) * P],
                                                ident[:].unsqueeze(1).broadcast_to([P, 4, P]), ALU.subtract)\
                            .then_inc(band_done, 1)
                    natural("sb_vu", vu, pairs=[0])
                    pl = plan["sb_sum"]
                    for h in range(SBH):
                        dve.wait_ge(work_full[WORK + h], pl["rf"] + 1)
                        nc.vector.tensor_tensor(zs[:, h, :], zs[:, h, :], ps[:, WORK + h, 0:384], ALU.subtract)\
                            .then_inc(w_log, 1)
                        dve.wait_ge(w_log, h + 1)
                        dve.sem_inc(bank_free[WORK + h], 1)
                    natural("sb_vu", vu, pairs=[1])
                    rest_tiles("sb_pv", [WORK + h for h in range(SBH)], 0)
                    pl = plan["pool_mean"]
                    for b in (5, 7):
                        dve.wait_ge(work_full[b], pl["rf"] + 1)
                        nc.vector.tensor_copy(pooled[:, 2 * (b - WORK):2 * (b - WORK) + 2, :],
                                              ps[:, b, :].rearrange("p (k t) -> p k t", t=T))\
                            .then_inc(bank_free[b], 1)
                    rest_tiles("pool_map", [WORK + g for g in range(4)], 8, scale=vec[:, 0:8])
                else:
                    transposed("gla_qk", qk)
                    dve.wait_ge(gw_done, 1)
                    nc.vector.tensor_tensor(gw_lo[:], gw_raw[:], gw_hi[:].bitcast(F32), ALU.subtract)\
                        .then_inc(gw_done, 1)
                    for m in range(MT):
                        dve.wait_ge(work_full[WORK + m], plan["gla_a"]["rf"] + 1)
                        nc.vector.tensor_copy(a_nat[:, m, :], ps[:, WORK + m, 0:RANK])\
                            .then_inc(bank_free[WORK + m], 1)
                    dve.wait_ge(work_full[4], plan["gla_at"]["rf"] + 1)
                    nc.vector.tensor_copy(a_t[0:RANK, :], ps[0:RANK, 4, 0:T]).then_inc(bank_free[4], 1)
                    pl = plan["gla_g"]
                    dve.wait_ge(g_done, 8)
                    for t in range(8):
                        b, j = WORK + t // 2, t % 2
                        ins = nc.vector.tensor_scalar(gate_u[:, t, :], ps[:, b, j * T:(j + 1) * T],
                                                      vec[:, 8 + t:9 + t], 0.0, ALU.add, ALU.min)
                        if j:
                            ins.then_inc(bank_free[b], 1)
                    dve.wait_ge(bank_free[7], pl["r"] + 2)
                    dve.wait_ge(g_done, 9)
                    then(nc.vector.tensor_tensor(gate_u[:], gate_u[:], gb[:].rearrange("p k c t -> p k (c t)"),
                                                 ALU.subtract))
                    dve.wait_ge(pool_step, 3)
                    for t in range(8):
                        ins = nc.vector.tensor_tensor_scan(
                            gb[:, t, :, :].rearrange("p c t -> p (c t)"), scan_m[:].rearrange("p c t -> p (c t)"),
                            gate_u[:, t, :], 0.0, ALU.mult, ALU.add)
                        then(ins)
                    def fours(tns):
                        return tns[:].rearrange("p k c t -> p (k c) t")
                    bc = lambda col: fours(gb)[:, :, col:col + 1].broadcast_to([P, 8 * NCH, CH])
                    nc.vector.tensor_tensor(fours(gla_e), fours(gb), bc(CH // 2), ALU.subtract)\
                        .then_inc(gate_done, 1)
                    qt = qk[:, 0:8, :].rearrange("p k t -> p (k t)")
                    kt_ = qk[:, 8:16, :].rearrange("p k t -> p (k t)")
                    flat = lambda tns: tns[:].rearrange("p k c t -> p (k c t)")

                    def state_gates():
                        dve.wait_ge(e_done, 1)
                        nc.vector.tensor_tensor(fours(gla_e), bc(CH - 1), fours(gb), ALU.subtract)\
                            .then_inc(e_used, 1)

                    def chunk_forms():
                        nc.vector.scalar_tensor_tensor(out=flat(qi), in0=flat(qi), scalar=GK ** -0.5, in1=qt,
                                                       op0=ALU.mult, op1=ALU.mult)
                        nc.vector.tensor_tensor(flat(ki), flat(ki), kt_, ALU.mult)
                        dve.wait_ge(e_done, 3)
                        nc.vector.tensor_tensor(kt_, kt_, flat(gla_e), ALU.mult).then_inc(e_used, 1)

                    def state_queries():
                        dve.wait_ge(e_done, 4)
                        then(nc.vector.scalar_tensor_tensor(out=qt, in0=flat(gla_e), scalar=GK ** -0.5, in1=qt,
                                                            op0=ALU.mult, op1=ALU.mult))

                    def decayed_queries():
                        then(nc.vector.tensor_tensor(dec3[:].unsqueeze(2), dec[:, :, 1:2], dec[:, :, 2:3],
                                                     ALU.mult))
                        q4 = qk[:, 0:8, :].rearrange("p k (c t) -> p k c t", t=CH)
                        for j, (cq, d) in enumerate(((2, dec[:, :, 1:2]), (3, dec[:, :, 2:3]),
                                                     (3, dec3[:].unsqueeze(2)))):
                            ins = nc.vector.tensor_tensor(qd[:, j, :, :], q4[:, :, cq, :],
                                                          d.broadcast_to([P, 8, CH]), ALU.mult)
                        ins.then_inc(e_used, 1)
                    natural("gla_v", gv, pairs=[0], mid=state_gates, end=chunk_forms)
                    natural("gla_v", gv, pairs=[1], mid=state_queries, end=decayed_queries)
                    pair(plan["gla_r"]["c"], nothing, nothing, nothing, nothing)
                    pl = plan["gla_o"]
                    for h in range(GH):
                        for m in range(MT):
                            b = WORK + 2 * (h % 2) + m
                            dve.wait_ge(work_full[b], pl["rf"] + h // 2 + 1)
                            nc.vector.tensor_copy(y[:, m, h * GV:(h + 1) * GV], ps[:, b, :])\
                                .then_inc(o_copied, 1)
                    for b in range(WORK, 8):
                        dve.wait_ge(bank_free[b], pl["r"] + 3)
                    nc.vector.tensor_scalar(ovar[:], ossq[:], 1.0 / GV, EPS, ALU.mult, ALU.add)\
                        .then_inc(osq_done, 1)
                    dve.wait_ge(oroot_done, 1)
                    dve.wait_ge(gla_in, 16 * 3)
                    for h in range(GH):
                        for m in range(MT):
                            cols = slice(h * GV, (h + 1) * GV)
                            ins = nc.vector.scalar_tensor_tensor(
                                out=y[:, m, cols], in0=y[:, m, cols], scalar=orstd[:, 2 * h + m:2 * h + m + 1],
                                in1=gnorm_sb[:], op0=ALU.mult, op1=ALU.mult)
                    ins.then_inc(gnorm_used, 1)

                    def times_gate(cols, quads):
                        def run():
                            dve.wait_ge(gnorm_used, 1)
                            for b, n in quads:
                                dve.wait_ge(bank_free[b], plan["gla_r"]["u"] + 1 + n)
                            for m in range(MT):
                                nc.vector.tensor_tensor(y[:, m, cols], y[:, m, cols], gr[:, m, cols], ALU.mult)\
                                    .then_inc(o_done, 1)
                        return run
                    pair(plan["gla_r"]["c"] + 8, nothing,
                         times_gate(slice(0, 3 * NB), ((0, 2), (1, 2), (2, 1), (3, 1))),
                         times_gate(slice(3 * NB, 4 * NB), ((2, 2), (3, 2))), nothing)
                    for m in range(MT):
                        rest_transposes("gla_t", m)
                output(f"mix_out{l}", f"pre_x{l}")
                transposed(f"xq{l}", qx)
                pl = plan[f"x_s{l}"]
                for h in range(XH + 1):
                    if h < XH:
                        dve.wait_ge(work_full[WORK + h], pl["rf"] + 1)
                        then(nc.vector.tensor_reduce(xden[:, h, :],
                                                     ps[:, WORK + h, :].rearrange("p (m t) -> p m t", t=T),
                                                     AX_X, ALU.max))
                        nc.vector.tensor_scalar(xmax[:, h, :], xden[:, h, :], -XD ** -0.5, None, ALU.mult)\
                            .then_inc(max_done, MT)
                    if h > 0:
                        dve.wait_ge(exp_done, (l * XH + h - 1) * MT + 2)
                        then(nc.vector.reciprocal(xrec[:, h - 1, :], xden[:, h - 1, :]))
                        for m in range(MT):
                            nc.vector.tensor_scalar(px[:, h - 1, m, :], px[:, h - 1, m, :],
                                                    xrec[:, h - 1, m:m + 1], None, ALU.mult).then_inc(p_done, 1)
                pl = plan[f"x_pt{l}"]
                for b in (5, 7):
                    dve.wait_ge(work_full[7], pl["rf"] + 1)
                    nc.vector.tensor_copy(pxt[:, b - WORK, :, :],
                                          ps[:, b, :].rearrange("p (k t) -> p k t", t=T))\
                        .then_inc(bank_free[b], 1)
                rest_tiles(f"x_pv{l}", [WORK + k % 4 for k in range(8)], 0)
                output(f"x_out{l}", f"pre_ff{l}")
                pl = plan[f"gu{l}"]
                def times_up(i):
                    def run():
                        for m in range(MT):
                            dve.wait_ge(bank_free[m], i + (pl["u"] + 2))
                            if m == 0:
                                dve.wait_ge(m0_done, i * 2 + (pl["a"] + 2))
                            else:
                                dve.wait_ge(w_used, i * 8 + (pl["c"] + 8 + W_SLOTS))
                            dve.wait_ge(work_full[7], i + pl["rf"])
                            nc.vector.tensor_tensor(nat[:, 0, m, :], ps[:, 2 + m, :], nat[:, 1, m, :], ALU.mult)\
                                .then_inc(bank_free[2 + m], 1)
                    return run

                def take_mid(i, k=0):
                    def run():
                        for b in (5, 7):
                            dve.wait_ge(work_full[b], i + (pl["rf"] + 1 - k))
                            nc.vector.tensor_copy(mid[:, bass.ds(i * 4 + (b - WORK - 4 * k), 1), :],
                                                  ps[:, b:b + 1, 0:T]).then_inc(bank_free[b], 1)
                    return run
                pair(pl["c"], nothing, nothing, times_up(0), nothing)
                with dve.Fori(1, FF // NB) as i:
                    pair(i * 8 + pl["c"], nothing, nothing, times_up(i), nothing, take_mid(i, 1))
                take_mid(FF // NB - 1)()
                pl = plan[f"down{l}"]
                jit0 = l * FT

                def jit(i, s):
                    dve.wait_ge(jit_hi, i * 4 + (jit0 + s + 1))
                    nc.vector.tensor_tensor(act_lo[:, s % 4:s % 4 + 1, :], mid[:, bass.ds(i * 4 + s, 1), :],
                                            act_hi[:, s % 4:s % 4 + 1, :].bitcast(F32), ALU.subtract)\
                        .then_inc(jit_done, 1)
                for s in range(4):
                    dve.wait_ge(jit_hi, jit0 + s + 1)
                    nc.vector.tensor_tensor(act_lo[:, s, :], mid[:, s, :], act_hi[:, s, :].bitcast(F32),
                                            ALU.subtract).then_inc(jit_done, 1)
                with dve.Fori(0, FT // 4 - 1) as i:
                    for s in range(4):
                        jit(i, s + 4)
                        split(i * 4 + pl["c"], s + 4)
                gain_ready()
                more = l < LAYERS - 1
                turn(pl["c"] + FT if more else None,
                     [[(4 * m + n, n * NB) for n in range(4)] for m in range(MT)],
                     [(m0_done, pl["a"] + 1), (w_used, pl["c"] + FT + W_SLOTS)],
                     [[(bank_free[n], pl["u"] + 2) for n in range(4)],
                      [(bank_free[4 + n], pl["r"] + 2) for n in range(4)]],
                     f"pre_mix{l + 1}" if more else None)

        @block.tensor
        def _(pe):
            pe.sem_inc(w_used, W_SLOTS)
            for b in range(8):
                pe.sem_inc(bank_free[b], 1)

            def mm(dst, lhs, rhs, start=True, stop=True, loose=False):
                return nc.tensor.matmul(dst, lhs, rhs, start=start, stop=stop, skip_group_check=loose)

            def skip(b, pl, k=0):
                pe.wait_ge(bank_free[b], pl["r"] + k + 1)
                pe.sem_inc(bank_free[b], 1)
                pe.sem_inc(work_full[b], 1)

            def emptied(b, pl, k=0):
                pe.wait_ge(bank_free[b], pl["r"] + k + 1)

            def mms(kt, m, s, k, dst):
                tok, wcols = slice(m * P, (m + 1) * P), slice(k * NB, (k + 1) * NB)
                mm(dst, act_hi[:, kt, tok], w_hi[:, s, wcols], kt == 0, False)
                mm(dst, act_hi[:, kt, tok], w_lo[:, s, wcols], False, False)
                return mm(dst, act_lo[:, kt, tok], w_hi[:, s, wcols], False, kt == KT - 1)

            def quad_by_tile(c, use, q, ready=None, transpose_m=None):
                if transpose_m is not None:
                    transpose_m(0)
                for m in range(MT):
                    pe.wait_ge(bank_free[2 * q + m], use)
                    for s in range(4):
                        if m == 0:
                            pe.wait_ge(lo_done, c * 2 + (2 * (4 * q + s + 1) + RAW_SLOTS))
                            if s == 3 and transpose_m is not None:
                                transpose_m(1)
                        if ready is not None:
                            ready(s, m)
                        for k in range(4):
                            last = mms(4 * s + k, m, s, k, ps[:, 2 * q + m, :])
                        if m == MT - 1:
                            last.then_inc(w_used, 1)
                        elif s == 3:
                            last.then_inc(m0_done, 1)

            def quad(c, use, q, after_first=None):
                for m in range(MT):
                    pe.wait_ge(bank_free[2 * q + m], use)
                for s in range(4):
                    pe.wait_ge(lo_done, c * 2 + (2 * (4 * q + s + 1) + RAW_SLOTS))
                    if s == 1 and after_first is not None:
                        after_first()
                    order = [(k, m) for k in range(4) for m in range(MT)] if s < 3 else \
                        [(k, m) for m in range(MT) for k in range(4)]
                    for k, m in order:
                        last = mms(4 * s + k, m, s, k, ps[:, 2 * q + m, :])
                        if s == 3 and k == 3 and m == 0:
                            last.then_inc(m0_done, 1)
                    last.then_inc(w_used, 1)

            def transpose_quad(i, pl, q):
                use = i + pl["u"] + 2
                for m in range(MT):
                    pe.wait_ge(bank_free[2 * q + m], use)
                for k in range(4):
                    b = WORK + 2 * q + k // 2
                    if k % 2 == 0:
                        pe.wait_ge(bank_free[b], i + (pl["r"] + 1))
                    for m in range(MT):
                        ins = nc.tensor.transpose(ps[:, b, (k % 2) * T + m * P:(k % 2) * T + (m + 1) * P],
                                                  nat[:, q, m, k * P:(k + 1) * P], ident[:])
                    if k % 2:
                        ins.then_inc(work_full[b], 1)

            def transposes(name, ready_sem, n0):
                pl = plan[name]

                def run(m):
                    pe.wait_ge(ready_sem, n0 + m + 1)
                    for b in range(4):
                        emptied(WORK + b, pl, m)
                        for k in range(4):
                            ins = nc.tensor.transpose(ps[:, WORK + b, k * P:(k + 1) * P],
                                                      y[:, m, (4 * b + k) * P:(4 * b + k + 1) * P], ident[:])
                        ins.then_inc(work_full[WORK + b], 1)
                return run

            def opening(name, source, ready_sem, n0):
                pl, src = plan[name], plan[source]

                def ready(s, m):
                    pe.wait_ge(bank_free[WORK + s], src["r"] + m + 2)
                quad_by_tile(pl["c"], pl["u"] + 1, 0, ready, transposes(source, ready_sem, n0))

            def transposed(name, source=None):
                pl = plan[name]

                def second(i):
                    quad(i * 8 + pl["c"], i + (pl["u"] + 1), 1, lambda: transpose_quad(i, pl, 0))
                    transpose_quad(i, pl, 1)
                if source is None:
                    with pe.Fori(0, 2) as i:
                        quad(i * 8 + pl["c"], i + (pl["u"] + 1), 0)
                        second(i)
                else:
                    opening(name, source, h_done, 2 * NORMS.index(source))
                    second(0)
                    quad(8 + pl["c"], 1 + (pl["u"] + 1), 0)
                    second(1)

            def natural(name, pairs=None):
                pl = plan[name]

                def one(i):
                    for q in range(2):
                        quad(i * 8 + pl["c"], i + (pl["u"] + 1), q)
                if pairs is None:
                    with pe.Fori(0, 2) as i:
                        one(i)
                else:
                    for i in pairs:
                        one(i)

            def output(name, opened=False):
                pl = plan[name]
                if not opened:
                    quad(pl["c"], pl["u"] + 1, 0)
                quad(pl["c"], pl["u"] + 1, 1)
                quad(pl["c"] + 8, pl["u"] + 2, 0)
                quad_by_tile(pl["c"] + 8, pl["u"] + 2, 1)

            def act_ready(name, rounds):
                pe.wait_ge(bank_free[7], plan[name]["r"] + rounds + 1)

            pe.wait_ge(consts_done, 4)
            for l in range(LAYERS):
                transposed(f"mk{l}", "mem_norm" if l == 0 else None)
                natural(f"mv{l}")
            pe.wait_ge(small_in, 32)
            emptied(4, plan["vec"])
            mm(ps[:, 4, 0:16], vec_rows[0:16, :], ident[0:16, 0:16]).then_inc(work_full[4], 1)
            for b in (5, 6, 7):
                skip(b, plan["vec"])
            for l in range(LAYERS):
                if l == 0:
                    transposed("sb_qk", "pre_mix0")
                    pl = plan["sb_z"]
                    for b in range(WORK, 8):
                        emptied(b, pl)
                    for h in range(SBH):
                        b = WORK + h
                        for dst, q_from, k_tile in ((slice(0, T), 0, 0), (slice(T, 384), P, 1)):
                            for d in range(2):
                                ins = mm(ps[:, b, dst], qk[:, 8 + 2 * h + d, k_tile * P:(k_tile + 1) * P],
                                         qk[:, 2 * h + d, q_from:T], d == 0, d == 1)
                        ins.then_inc(work_full[b], 1)
                    natural("sb_vu", pairs=[0])
                    pl = plan["sb_sum"]
                    pe.wait_ge(sp_done, 1)
                    for h in range(SBH):
                        b = WORK + h
                        emptied(b, pl)
                        mm(ps[:, b, 0:P], tri[:], sp_t[:, h, 0:P])
                        mm(ps[:, b, P:T], tri[:], sp_t[:, h, P:T], True, False)
                        mm(ps[:, b, P:T], ones[:], sp_t[:, h, T:384], False, True)
                        mm(ps[:, b, T:384], tri[:], sp_t[:, h, T:384]).then_inc(work_full[b], 1)
                    natural("sb_vu", pairs=[1])
                    pl = plan["sb_pv"]
                    pe.wait_ge(w_done, 1)
                    for b in range(4):
                        pe.wait_ge(bank_free[b], plan["sb_vu"]["u"] + 3)
                    for h in range(SBH):
                        b = WORK + h
                        emptied(b, pl)
                        for d in range(2):
                            f = slice((2 * h + d) * P, (2 * h + d + 1) * P)
                            mm(ps[:, b, d * T:(d + 1) * T], vu[:, 0, f], zs[:, h, 0:T], True, False)
                            ins = mm(ps[:, b, d * T + P:(d + 1) * T], vu[:, 1, f], zs[:, h, T:384], False, True)
                        ins.then_inc(work_full[b], 1)
                    pl = plan["pool_mean"]
                    pe.wait_ge(band_done, MT)
                    for g in range(4):
                        b = WORK + g
                        emptied(b, pl)
                        for d in range(2):
                            f = slice(SBW + (2 * g + d) * P, SBW + (2 * g + d + 1) * P)
                            for k in range(MT):
                                ins = mm(ps[:, b, d * T:(d + 1) * T], vu[:, k, f], band[:, g, k, :],
                                         k == 0, k == MT - 1)
                        ins.then_inc(work_full[b], 1)
                    pl = plan["pool_map"]
                    pe.wait_ge(pw_in, 64)
                    for b in range(WORK, 8):
                        emptied(b, pl)
                    for g in range(4):
                        b = WORK + g
                        for d in range(2):
                            for k in range(2):
                                ins = mm(ps[:, b, d * T:(d + 1) * T], pw[:, g, k, d * P:(d + 1) * P],
                                         pooled[:, 2 * g + k, :], k == 0, k == 1)
                        ins.then_inc(work_full[b], 1)
                    act_ready("pool_map", 1)
                else:
                    transposed("gla_qk", "pre_mix1")
                    pl = plan["gla_a"]
                    pe.wait_ge(gw_done, 2)
                    for m in range(MT):
                        emptied(WORK + m, pl)
                        for kt in range(KT):
                            tok = slice(m * P, (m + 1) * P)
                            dst = ps[:, WORK + m, 0:RANK]
                            mm(dst, act_hi[:, kt, tok], gw_hi[:, kt, :], kt == 0, False)
                            mm(dst, act_hi[:, kt, tok], gw_lo[:, kt, :], False, False)
                            ins = mm(dst, act_lo[:, kt, tok], gw_hi[:, kt, :], False, kt == KT - 1)
                        ins.then_inc(work_full[WORK + m], 1)
                    for b in (6, 7):
                        skip(b, pl)
                    pl = plan["gla_at"]
                    emptied(4, pl)
                    emptied(5, pl)
                    for m in range(MT):
                        ins = mm(ps[0:RANK, 4, m * P:(m + 1) * P], a_nat[:, m, :], ident[:])
                    ins.then_inc(work_full[4], 1)
                    for b in (5, 6, 7):
                        skip(b, pl)
                    pl = plan["gla_g"]
                    pe.wait_ge(gla_in, 16 * 3)
                    for b in range(WORK, 8):
                        emptied(b, pl)
                    for t in range(8):
                        b, j = WORK + t // 2, t % 2
                        ins = mm(ps[:, b, j * T:(j + 1) * T], gate_w_sb[0:RANK, t * P:(t + 1) * P], a_t[0:RANK, :])
                        if j:
                            ins.then_inc(work_full[b], 1)
                    natural("gla_v")
                    pl = plan["gla_s"]
                    pe.wait_ge(e_used, 3)
                    decayed = {(0, 2): 0, (1, 3): 1, (0, 3): 2}
                    for h in range(GH):
                        b = WORK + h
                        emptied(b, pl)
                        for ck in range(NCH):
                            for cq in range(2 * (ck // 2), NCH):
                                rows = slice(CH * (ck % 2), CH * (ck % 2 + 1))
                                col = (ck // 2) * T + cq * CH
                                for d in range(2):
                                    t = 2 * h + d
                                    if ck >= cq:
                                        lhs, rhs = ki[:, t, ck, :], qi[:, t, cq, :]
                                    else:
                                        lhs = qk[:, 8 + t, ck * CH:(ck + 1) * CH]
                                        rhs = qk[:, t, cq * CH:(cq + 1) * CH] if cq == ck + 1 else \
                                            qd[:, decayed[ck, cq], t, :]
                                    ins = mm(ps[rows, b, col:col + CH], lhs, rhs, d == 0, d == 1)
                        ins.then_inc(work_full[b], 1)
                    natural("gla_r", pairs=[0])
                    pl = plan["gla_o"]
                    pe.wait_ge(sc_done, 2)
                    for h in range(GH):
                        for m in range(MT):
                            b = WORK + 2 * (h % 2) + m
                            emptied(b, pl, h // 2)
                            for k in range(m + 1):
                                ins = mm(ps[:, b, :], gla_sc[:, h, k, m * P:(m + 1) * P],
                                         gv[:, k, h * GV:(h + 1) * GV], k == 0, k == m)
                            ins.then_inc(work_full[b], 1)
                    natural("gla_r", pairs=[1])
                    opening("mix_out1", "gla_t", o_done, MT)
                output(f"mix_out{l}", opened=l == 1)
                transposed(f"xq{l}", f"pre_x{l}")
                pl = plan[f"x_s{l}"]
                pe.wait_ge(kv_in, 32 * (l + 1))
                for b in range(WORK, 8):
                    emptied(b, pl)
                for h in range(XH):
                    b = WORK + h
                    for m in range(MT):
                        for d in range(4):
                            ins = mm(ps[:, b, m * T:(m + 1) * T], qx[:, 4 * h + d, m * P:(m + 1) * P],
                                     kx[:, 4 * h + d, :], d == 0, d == 3)
                    ins.then_inc(work_full[b], 1)
                pl = plan[f"x_pt{l}"]
                for h in range(XH):
                    b = WORK + h
                    pe.wait_ge(p_done, (l * XH + h) * MT + 2)
                    emptied(b, pl)
                    for k in range(2):
                        for m in range(MT):
                            ins = nc.tensor.transpose(ps[:, b, k * T + m * P:k * T + (m + 1) * P],
                                                      px[:, h, m, k * P:(k + 1) * P], ident[:])
                    ins.then_inc(work_full[b], 1)
                pl = plan[f"x_pv{l}"]
                for b in range(WORK, 8):
                    emptied(b, pl)
                for g in range(8):
                    b = WORK + g % 4
                    emptied(b, pl, g // 4)
                    for d in range(2):
                        t = 2 * g + d
                        for k in range(2):
                            ins = mm(ps[:, b, d * T:(d + 1) * T], vx[:, k, t * P:(t + 1) * P],
                                     pxt[:, g // 2, k, :], k == 0, k == 1)
                    ins.then_inc(work_full[b], 1)
                act_ready(f"x_pv{l}", 2)
                output(f"x_out{l}")
                pl = plan[f"gu{l}"]
                def transpose_mid(i, k=0):
                    for m in range(MT):
                        pe.wait_ge(bank_free[2 + m], i + (pl["u"] + 2 - k))
                    for j in range(4):
                        b = WORK + j
                        pe.wait_ge(bank_free[b], i + (pl["r"] + 1 - k))
                        for m in range(MT):
                            ins = nc.tensor.transpose(ps[:, b, m * P:(m + 1) * P], nat[:, 0, m, j * P:(j + 1) * P],
                                                      ident[:])
                        ins.then_inc(work_full[b], 1)
                opening(f"gu{l}", f"pre_ff{l}", h_done, 2 * NORMS.index(f"pre_ff{l}"))
                quad(pl["c"], pl["u"] + 1, 1)
                with pe.Fori(1, FF // NB) as i:
                    quad(i * 8 + pl["c"], i + (pl["u"] + 1), 0, lambda: transpose_mid(i, 1))
                    quad(i * 8 + pl["c"], i + (pl["u"] + 1), 1)
                transpose_mid(FF // NB - 1)
                pl = plan[f"down{l}"]
                jit0 = l * FT

                def row_ready(i, s):
                    pe.wait_ge(lo_done, i * 8 + (2 * (pl["c"] + s + 1) + RAW_SLOTS))
                    pe.wait_ge(jit_done, i * 4 + (jit0 + s + 1))

                def row(s, m, start=False):
                    tok = slice(m * P, (m + 1) * P)
                    for a, w, st in ((act_hi, w_hi, start), (act_hi, w_lo, False), (act_lo, w_hi, False)):
                        for n in range(4):
                            ins = mm(ps[:, 4 * m + n, :], a[:, s, tok], w[:, s, n * NB:(n + 1) * NB],
                                     st, True, True)
                    return ins
                for b in range(4):
                    pe.wait_ge(bank_free[b], pl["u"] + 1)
                for b in range(WORK, 8):
                    emptied(b, pl)
                for s in range(4):
                    row_ready(0, s)
                    for m in range(MT):
                        last = row(s, m, s == 0)
                    last.then_inc(w_used, 1)
                with pe.Fori(1, FT // 4 - 1) as i:
                    for s in range(4):
                        row_ready(i, s)
                        for m in range(MT):
                            last = row(s, m)
                        last.then_inc(w_used, 1)
                for m in range(MT):
                    for s in range(4):
                        if m == 0:
                            row_ready(FT // 4 - 1, s)
                        last = row(s, m)
                        if m == MT - 1:
                            last.then_inc(w_used, 1)
                        elif s == 3:
                            last.then_inc(m0_done, 1)


_INS = ["x", "mem", "norms", "mem_norm", "even_w_in", "pool_w", "pool_scale", "even_w_out", "odd_w_in",
        "gla_gate_w", "gla_gate_b", "gla_gnorm", "odd_w_out", "xattn_wq", "xattn_wk", "xattn_wv", "xattn_wo",
        "ffn_w_gate", "ffn_w_up", "ffn_w_down"]
_FIRST_ONLY = {"x", "mem", "even_w_in", "pool_w", "pool_scale", "even_w_out", "odd_w_in", "gla_gate_w",
               "gla_gate_b", "gla_gnorm", "odd_w_out"}


def kernel(**inputs):
    import numpy as np
    import concourse.bacc as bacc
    from concourse.bass_utils import run_bass_kernel_spmd

    nc = bacc.Bacc("TRN2", target_bir_lowering=False, num_devices=1)
    arrays, args = {}, []
    for name in _INS:
        a = np.ascontiguousarray(inputs[name])
        arrays[f"in_{name}"] = a
        ap = nc.dram_tensor(f"in_{name}", a.shape, mybir.dt.from_np(a.dtype), kind="ExternalInput").ap()
        args.append(ap[0] if name in _FIRST_ONLY else ap)
    shape = inputs["x"].shape
    out = nc.dram_tensor("out", shape, F32, kind="ExternalOutput").ap()
    build(nc, *args, out[0])
    r = run_bass_kernel_spmd(nc, [arrays], core_ids=[0])
    return r.results[0]["out"]
```
